# Optimizing a Trainium2 kernel written in Bass

```python
import math
import jax, jax.numpy as jnp
from jax import lax
import numpy as np

D_MODEL = 1024
BATCH = 1
SEQ = 512
DEPTH = 2

SB_HEADS = 8
SB_HEAD_DIM = 64
SB_WIDTH = SB_HEADS * SB_HEAD_DIM
DIFF_HEADS = 4
DIFF_QK_DIM = 64
DIFF_V_DIM = 2 * DIFF_QK_DIM
DIFF_QK_WIDTH = DIFF_HEADS * 2 * DIFF_QK_DIM
DIFF_V_WIDTH = DIFF_HEADS * DIFF_V_DIM
ROPE_THETA = 500000.0
ROT_DIM = DIFF_QK_DIM // 4
Q_BLOCK = 128
IN_COLS = 3 * SB_WIDTH + 2 * DIFF_QK_WIDTH + DIFF_V_WIDTH + 2 * D_MODEL
PEER_HEADS = 8
PEER_N_KEYS = 128
PEER_N_EXPERTS = PEER_N_KEYS * PEER_N_KEYS
PEER_TOPK = 16
PEER_QUERY_DIM = 256
PEER_HALF_DIM = PEER_QUERY_DIM // 2
PEER_CHUNK = 128
NORM_EPS = 1e-6

kernel_name = "hybrid_sb_diffattn_peer_adaln"

def rmsnorm(x, g):
    xf = x.astype(jnp.float32)
    y = xf * lax.rsqrt(jnp.mean(xf * xf, axis=-1, keepdims=True) + NORM_EPS)
    return (y * g.astype(jnp.float32)).astype(x.dtype)

def rope_tables(seq_len):
    pos = jnp.arange(seq_len, dtype=jnp.float32)
    inv_freq = 1.0 / (ROPE_THETA ** (jnp.arange(0, ROT_DIM, 2, dtype=jnp.float32) / ROT_DIM))
    ang = pos[:, None] * inv_freq[None, :]
    return jnp.cos(ang), jnp.sin(ang)

def partial_rope(t, cos, sin):
    tf = t.astype(jnp.float32)
    half = ROT_DIM // 2
    t1 = tf[..., :half]
    t2 = tf[..., half:ROT_DIM]
    rot = jnp.concatenate([t1 * cos - t2 * sin, t2 * cos + t1 * sin], axis=-1)
    return jnp.concatenate([rot, tf[..., ROT_DIM:]], axis=-1).astype(t.dtype)

def stick_breaking_attention(q, k, v):
    B, H, S, d = q.shape
    nb = S // Q_BLOCK
    qb = q.reshape(B, H, nb, Q_BLOCK, d).transpose(2, 0, 1, 3, 4)
    kf = k.astype(jnp.float32)
    vf = v.astype(jnp.float32)
    key_pos = jnp.arange(S)
    scale = 1.0 / math.sqrt(d)

    def block(args):
        qi, i = args
        z = jnp.einsum('bhqd,bhkd->bhqk', qi.astype(jnp.float32), kf) * scale
        q_pos = i * Q_BLOCK + jnp.arange(Q_BLOCK)
        mask = key_pos[None, :] < q_pos[:, None]
        log_fail = jnp.where(mask, jax.nn.log_sigmoid(-z), 0.0)
        after = lax.cumsum(log_fail, axis=3, reverse=True) - log_fail
        w = jnp.where(mask, jnp.exp(jax.nn.log_sigmoid(z) + after), 0.0)
        return jnp.einsum('bhqk,bhkd->bhqd', w, vf)

    out = lax.map(block, (qb, jnp.arange(nb)))
    return out.transpose(1, 2, 0, 3, 4).reshape(B, H, S, d).astype(v.dtype)

def diff_attention(q, k, v, lam):
    B, H, _, S, d = q.shape
    dv = v.shape[-1]
    nb = S // Q_BLOCK
    qb = q.reshape(B, H, 2, nb, Q_BLOCK, d).transpose(3, 0, 1, 2, 4, 5)
    kf = k.astype(jnp.float32)
    vf = v.astype(jnp.float32)
    key_pos = jnp.arange(S)
    scale = 1.0 / math.sqrt(d)

    def block(args):
        qi, i = args
        s = jnp.einsum('bhcqd,bhckd->bhcqk', qi.astype(jnp.float32), kf) * scale
        q_pos = i * Q_BLOCK + jnp.arange(Q_BLOCK)
        mask = key_pos[None, :] <= q_pos[:, None]
        p = jax.nn.softmax(jnp.where(mask, s, -jnp.inf), axis=-1)
        w = p[:, :, 0] - lam * p[:, :, 1]
        return jnp.einsum('bhqk,bhkd->bhqd', w, vf)

    out = lax.map(block, (qb, jnp.arange(nb)))
    return out.transpose(1, 2, 0, 3, 4).reshape(B, H, S, dv).astype(v.dtype)

def token_mixer(h, w_in, gate_b, lam_params, subln_g, w_b_sb, w_b_diff, w_out, cos, sin, lam_init):
    B, S, _ = h.shape
    proj = h @ w_in
    sizes = [SB_WIDTH, SB_WIDTH, SB_WIDTH, DIFF_QK_WIDTH, DIFF_QK_WIDTH, DIFF_V_WIDTH, D_MODEL]
    splits = [int(s) for s in np.cumsum(sizes)]
    sb_q, sb_k, sb_v, d_q, d_k, d_v, g_sb_pre, g_diff_pre = jnp.split(proj, splits, axis=-1)

    def heads(t, n, d):
        return t.reshape(B, S, n, d).transpose(0, 2, 1, 3)

    y_sb = stick_breaking_attention(heads(sb_q, SB_HEADS, SB_HEAD_DIM),
                                    heads(sb_k, SB_HEADS, SB_HEAD_DIM),
                                    heads(sb_v, SB_HEADS, SB_HEAD_DIM))
    y_sb = y_sb.transpose(0, 2, 1, 3).reshape(B, S, SB_WIDTH)

    dq = d_q.reshape(B, S, DIFF_HEADS, 2, DIFF_QK_DIM).transpose(0, 2, 3, 1, 4)
    dk = d_k.reshape(B, S, DIFF_HEADS, 2, DIFF_QK_DIM).transpose(0, 2, 3, 1, 4)
    dq = partial_rope(dq, cos, sin)
    dk = partial_rope(dk, cos, sin)
    lp = lam_params.astype(jnp.float32)
    lam = jnp.exp(jnp.sum(lp[0] * lp[1])) - jnp.exp(jnp.sum(lp[2] * lp[3])) + lam_init
    y_diff = diff_attention(dq, dk, heads(d_v, DIFF_HEADS, DIFF_V_DIM), lam)
    y_diff = rmsnorm(y_diff, subln_g) * (1.0 - lam_init)
    y_diff = y_diff.transpose(0, 2, 1, 3).reshape(B, S, DIFF_V_WIDTH)

    g_sb = jax.nn.sigmoid(g_sb_pre + gate_b[:D_MODEL])
    g_diff = jax.nn.sigmoid(g_diff_pre + gate_b[D_MODEL:])
    merged = g_sb * (y_sb @ w_b_sb) + g_diff * (y_diff @ w_b_diff)
    return merged @ w_out

def peer_mixer(h, wq, subkeys, u, v):
    B, S, D = h.shape
    q = (h @ wq).astype(jnp.float32).reshape(B, S, PEER_HEADS, 2, PEER_HALF_DIM)
    scores = jnp.einsum('bshcd,hcnd->bshcn', q, subkeys.astype(jnp.float32))
    s_top, i_top = lax.top_k(scores, PEER_TOPK)
    cand = s_top[..., 0, :, None] + s_top[..., 1, None, :]
    cand_idx = i_top[..., 0, :, None] * PEER_N_KEYS + i_top[..., 1, None, :]
    cand = cand.reshape(B, S, PEER_HEADS, PEER_TOPK * PEER_TOPK)
    cand_idx = cand_idx.reshape(B, S, PEER_HEADS, PEER_TOPK * PEER_TOPK)
    best, pos = lax.top_k(cand, PEER_TOPK)
    expert_idx = jnp.take_along_axis(cand_idx, pos, axis=-1)
    gates = jax.nn.softmax(best, axis=-1)

    T = B * S
    E = PEER_HEADS * PEER_TOPK
    nc = T // PEER_CHUNK
    hc = h.reshape(nc, PEER_CHUNK, D)
    ic = expert_idx.reshape(nc, PEER_CHUNK, E)
    gc = gates.reshape(nc, PEER_CHUNK, E)

    def chunk(args):
        hh, ii, gg = args
        u_sel = jnp.take(u, ii, axis=0)
        a = jnp.einsum('cd,ced->ce', hh.astype(jnp.float32), u_sel.astype(jnp.float32))
        act = jax.nn.gelu(a, approximate=False) * gg
        v_sel = jnp.take(v, ii, axis=0)
        return jnp.einsum('ce,ced->cd', act, v_sel.astype(jnp.float32))

    out = lax.map(chunk, (hc, ic, gc))
    return out.reshape(B, S, D).astype(h.dtype)

def setup_inputs(seed: int = 0) -> dict:
    key = jax.random.key(seed)
    ks = jax.random.split(key, 20)
    f32 = jnp.float32
    D = D_MODEL
    nrm = lambda k, shape, s: jax.random.normal(k, shape, f32) * s
    return {
        "x": nrm(ks[0], (BATCH, SEQ, D), 1.0),
        "c": nrm(ks[1], (BATCH, D), 1.0),
        "norm1_g": 1.0 + nrm(ks[2], (DEPTH, D), 0.02),
        "norm2_g": 1.0 + nrm(ks[3], (DEPTH, D), 0.02),
        "ada_w": nrm(ks[4], (DEPTH, D, 6 * D), 0.5 * D ** -0.5),
        "ada_b": nrm(ks[5], (DEPTH, 6 * D), 0.02),
        "w_in": nrm(ks[6], (DEPTH, D, IN_COLS), D ** -0.5),
        "gate_b": nrm(ks[7], (DEPTH, 2 * D), 0.02),
        "diff_lambda": nrm(ks[8], (DEPTH, 4, DIFF_QK_DIM), 0.1),
        "diff_subln_g": 1.0 + nrm(ks[9], (DEPTH, DIFF_V_DIM), 0.02),
        "w_branch_sb": nrm(ks[10], (DEPTH, SB_WIDTH, D), SB_WIDTH ** -0.5),
        "w_branch_diff": nrm(ks[11], (DEPTH, DIFF_V_WIDTH, D), DIFF_V_WIDTH ** -0.5),
        "w_out": nrm(ks[12], (DEPTH, D, D), D ** -0.5),
        "peer_wq": nrm(ks[13], (DEPTH, D, PEER_HEADS * PEER_QUERY_DIM), D ** -0.5),
        "peer_subkeys": nrm(ks[14], (DEPTH, PEER_HEADS, 2, PEER_N_KEYS, PEER_HALF_DIM), PEER_HALF_DIM ** -0.5),
        "peer_u": nrm(ks[15], (DEPTH, PEER_N_EXPERTS, D), D ** -0.5),
        "peer_v": nrm(ks[16], (DEPTH, PEER_N_EXPERTS, D), 1.0),
        "final_g": 1.0 + nrm(ks[17], (D,), 0.02),
    }

def reference(x, c, norm1_g, norm2_g, ada_w, ada_b, w_in, gate_b, diff_lambda, diff_subln_g,
              w_branch_sb, w_branch_diff, w_out, peer_wq, peer_subkeys, peer_u, peer_v, final_g):
    S = x.shape[1]
    cos, sin = rope_tables(S)
    c_act = jax.nn.silu(c)
    for i in range(DEPTH):
        lam_init = 0.8 - 0.6 * math.exp(-0.3 * i)
        mod = c_act @ ada_w[i] + ada_b[i]
        shift1, scale1, gate1, shift2, scale2, gate2 = jnp.split(mod[:, None, :], 6, axis=-1)
        h = rmsnorm(x, norm1_g[i]) * (1.0 + scale1) + shift1
        y = token_mixer(h, w_in[i], gate_b[i], diff_lambda[i], diff_subln_g[i],
                        w_branch_sb[i], w_branch_diff[i], w_out[i], cos, sin, lam_init)
        x = x + (gate1 * y).astype(x.dtype)
        h = rmsnorm(x, norm2_g[i]) * (1.0 + scale2) + shift2
        y = peer_mixer(h, peer_wq[i], peer_subkeys[i], peer_u[i], peer_v[i])
        x = x + (gate2 * y).astype(x.dtype)
    return rmsnorm(x, final_g)


_drawn_inputs = setup_inputs


def setup_inputs(seed=0):
    import zlib

    import numpy as np

    out = dict(_drawn_inputs(seed))
    spreads = {}
    factors = {'gate_b': 4.031, 'diff_subln_g': 3.279, 'final_g': 2.872}
    for name, (base, spread) in spreads.items():
        noise = np.random.default_rng([zlib.crc32(name.encode()), seed]).standard_normal(out[name].shape)
        drawn = base * np.exp(spread * noise) if base else spread * noise
        out[name] = __import__('jax').numpy.asarray(drawn.astype(out[name].dtype))
    for name, factor in factors.items():
        out[name] = (out[name] * factor).astype(out[name].dtype)
    return out
```

```python
import math
from contextlib import ExitStack

import numpy as np

import concourse.bass as bass
from concourse import mybir

F32 = mybir.dt.float32
U32 = mybir.dt.uint32
ALU = mybir.AluOpType
ACT = mybir.ActivationFunctionType
AX = mybir.AxisListType

P = 128
D = 1024
KD = D // P
SEQ = 512
CH = SEQ // P
DEPTH = 2
HD = 64
TURNS = 4
MT = D // P
N_KEYS = 128
N_EXPERTS = N_KEYS * N_KEYS
HEADS = 8
TOPK = 16
EPS = 1e-6
ROT = 16
ROPE_THETA = 500000.0
SCALE = 1.0 / math.sqrt(HD)
MOD_BLOCKS = 6 * D // 512
RING = 8
V_PE = 8
LOWEST = -3.0e38
LAM_INIT = [0.8 - 0.6 * math.exp(-0.3 * i) for i in range(DEPTH)]
IDENT, NEG_UPPER, NEG_ONES, STRICT, NEG_MASK, ROPE_PERM = range(6)
N_CONST = 6
Y_BANK = [6, 0, 1, 6]

A_WQKV = 0
A_SOFT = 6144
A_W = 7168
A_QKV = 8192
A_L = 12288
A_P = 16384
A_WT = 18432
A_YN = 19456
A_ROPE = 19712
A_YSB = 20736
A_YD = 22784
A_MERGED = 24832
A_SIG = 28928
A_WOUT = 0
A_MW = 12288
A_ADAW = 20736
A_ACC = 28928
A_BIAS = 29952
A_RING = 0
A_QW = 16384
A_QST = 18688
A_TOPK = 16384
A_SCORES = 19712
A_H2 = 28160
ARENA = 32256


def build(nc, io, out):
    with ExitStack() as ctx:
        def sb(name, shape, dt=F32):
            return ctx.enter_context(nc.sbuf_tensor(name, shape, dt))

        def sem(name):
            return ctx.enter_context(nc.semaphore(name))

        ps = ctx.enter_context(nc.psum_tensor("ps", [P, 8, 512], F32))
        x = sb("x_res", [P, CH, D])
        hT = sb("hT", [P, KD, SEQ])
        mod = sb("mod", [P, 6, D])
        g_row = sb("g_row", [P, D])
        h_tmp = sb("h_tmp", [P, D])
        h_row = sb("h_row", [P, D])
        const = sb("const", [P, N_CONST, P])
        ones = sb("ones", [P, P])
        cos_t = sb("cos_t", [P, SEQ])
        sin_t = sb("sin_t", [P, SEQ])
        c_raw = sb("c_raw", [P, KD])
        c_sig = sb("c_sig", [P, KD])
        c_act = sb("c_act", [P, KD])
        c_rep = sb("c_rep", [P, KD, P])
        lam_sum = sb("lam_sum", [P, 2])
        lam_exp = sb("lam_exp", [P, 2])
        lam_init = sb("lam_init", [P, DEPTH])
        lam_rest = sb("lam_rest", [P, DEPTH])
        neg_lam = sb("neg_lam", [P, 1])
        g_sub = sb("g_sub", [P, P])
        gate_b = sb("gate_b", [P, 2 * MT])
        ss = sb("ss", [P, 1])
        root0 = sb("root0", [P, 1])
        rstd = sb("rstd", [P, 1])
        newton = sb("newton", [P, 2])
        eps = sb("eps", [P, 1])
        nmax = sb("nmax", [P, 8])
        zsum = sb("zsum", [P, 8])
        rz = sb("rz", [P, 8])
        yss = sb("yss", [P, CH])
        yroot0 = sb("yroot0", [P, CH])
        yr = sb("yr", [P, CH])
        arena = sb("arena", [P, ARENA])

        def part(at, *dims):
            n = int(np.prod(dims))
            v = arena[:, at:at + n]
            if len(dims) == 2:
                v = v.rearrange("p (a b) -> p a b", a=dims[0])
            if len(dims) == 3:
                v = v.rearrange("p (a b c) -> p a b c", a=dims[0], b=dims[1])
            return v

        w_qkv = part(A_WQKV, 6, KD, P)
        soft = part(A_SOFT, 2, SEQ)
        junk = part(A_SOFT, D)
        junk_y = part(A_SOFT, P)
        lam_raw = part(A_W, 4, HD)
        lam_prod = part(A_W + 4 * HD, 2, HD)
        w_att = part(A_W, 2, SEQ)
        qkv = part(A_QKV, 8, SEQ)
        sb_q, sb_k, sb_v, dq_raw, dk_raw, dq, dk, d_v = (qkv[:, n, :] for n in range(8))
        L = part(A_L, 2, CH, SEQ)
        prob = part(A_P, 4, SEQ)
        w_t = part(A_WT, 2, SEQ)
        y_n = part(A_YN, 2, P)
        rope_tmp = part(A_ROPE, 2, SEQ)
        y_sb = part(A_YSB, TURNS, SEQ)
        y_d = part(A_YD, TURNS, SEQ)
        merged = part(A_MERGED, MT, SEQ)
        sig = part(A_SIG, 2, 2, SEQ)
        w_out = part(A_WOUT, KD, D)
        w_m = part(A_MW, 2, 24, P)
        ada_w = part(A_ADAW, 2, KD, 512)
        mod_acc = part(A_ACC, 2, 512)
        bias0 = part(A_BIAS, 2, 512)
        out_tmp = part(A_SIG, 512)
        q_w = part(A_QW, 2, KD + 1, P)
        q_st = part(A_QST, 2, SEQ)
        ring_u = part(A_RING, RING, D)
        ring_v = part(A_RING + RING * D, RING, D)
        scores = part(A_SCORES, CH * HEADS + 1, 2 * N_KEYS)
        h2 = part(A_H2, CH, D)
        at = [A_TOPK]

        def small(*dims):
            v = part(at[0], *dims)
            at[0] += int(np.prod(dims))
            assert at[0] <= A_SCORES
            return v

        sc_in = small(2, N_KEYS)
        sc_work = small(2, N_KEYS)
        cand = small(TOPK, TOPK)
        cand_work = small(TOPK, TOPK)
        onehot = small(TOPK, TOPK)
        s_top = small(2, TOPK)
        i_top_f = small(2, TOPK)
        best = small(TOPK)
        pos_f = small(2, TOPK)
        sel_f = small(2, TOPK)
        gexp = small(TOPK)
        gsum = small(1)
        rsum = small(1)
        nbest = small(1)
        dots = small(TOPK)
        gel = small(TOPK)
        coef = small(TOPK)
        diag = small(V_PE, P)
        i_top = sb("i_top", [P, 2, TOPK], U32)
        pos = sb("pos", [P, TOPK], U32)
        pos_hl = sb("pos_hl", [P, 2, TOPK], U32)
        idx_next = sb("idx_next", [P, TOPK], U32)
        idx_u = sb("idx_u", [P, TOPK], U32)
        idx_v = sb("idx_v", [P, TOPK], U32)
        iota16 = sb("iota16", [P, TOPK])
        expert0 = sb("expert0", [P, DEPTH])

        S = {n: sem(n) for n in (
            "const_in x_in c_sig_done c_act_done zeros_done layer_done small_in lam_summed lam_exped g_in "
            "norm_gain mod_mm mod_evac acc_ready sq_done norm_h tr_done hT_ev "
            "q_ev k_ev v_ev dqraw_ev dkraw_ev dv_ev rope_mm dq_ready dk_ready "
            "z_done  ln_done L_done b_done w_exp w_masked pv_done ysb_ev "
            "s_done max_done p_exp dw_done wt_done wt_ev y_done y_sq yn_done yt_done yd_ev "
            "sig_done merged_done wout_in wo_done x_upd "
            "query_done qst_ev sc_done sc_ev topk_done idx_taken gate_exp dots_done gelu_done coef_done diag_done "
            "idx_u_set u_used v_dve v_pe v_added out_sq out_ready "
            "parked_act parked_dve parked_pool parked_pe parked_sp").split()}
        ada_in = [sem(f"ada_in{i}") for i in range(2)]
        w_in = [sem(f"w_in{i}") for i in range(6)]
        proj = [sem(f"proj{i}") for i in range(6)]
        m_in = [sem(f"m_in{i}") for i in range(2)]
        m_mm = [sem(f"m_mm{i}") for i in range(2)]
        q_in = [sem(f"q_in{i}") for i in range(2)]
        out_done = [sem(f"out_done{i}") for i in range(2)]
        u_in = [sem(f"u_in{i}") for i in range(RING)]
        v_in = [sem(f"v_in{i}") for i in range(RING)]

        def wait(eng, name, value):
            eng.wait_ge(S[name], value)

        def C(n):
            return const[:, n, :]

        def qcols(kb):
            return SEQ - P * kb

        block = ctx.enter_context(nc.Block())

        @block.sync
        def _(sp):
            def park():
                sp.sem_inc(S["parked_sp"], 1)

            sp.dma_start(c_raw[:, :], io["c"]).then_inc(S["const_in"], 16)
            sp.dma_start(const[:, :, :], io["const"]).then_inc(S["const_in"], 16)
            sp.dma_start(cos_t[:, :], io["cos"]).then_inc(S["const_in"], 16)
            sp.dma_start(sin_t[:, :], io["sin"]).then_inc(S["const_in"], 16)
            sp.dma_start(iota16[:, :], io["iota16"].partition_broadcast(P)).then_inc(S["const_in"], 16)
            sp.dma_start(x[:, :, :], io["x"].rearrange("(c p) d -> p c d", p=P)).then_inc(S["x_in"], 16)

            def load_mod(l, lo, hi):
                with sp.Fori(lo, hi) as n2:
                    for s in range(2):
                        wait(sp, "mod_evac", l * MOD_BLOCKS + n2 * 2 + s + 1)
                        park()
                        sp.dma_start(ada_w[:, s], io["ada_w"][bass.ds(l * MOD_BLOCKS + n2 * 2 + s, 1)]
                                     .rearrange("a p k n -> p (a k) n")).then_inc(ada_in[s], 16)
                        sp.dma_start(bias0[0:1, s, :], io["ada_b"][bass.ds(l * MOD_BLOCKS + n2 * 2 + s, 1), :]
                                     ).then_inc(ada_in[s], 16)

            def load_g(l, which):
                wait(sp, "norm_gain", l * 2 + which + 1)
                park()
                sp.dma_start(g_row[:, :], io["norm_g"][bass.ds(l * 2 + which, 1), :]
                             .partition_broadcast(P).rearrange("p a d -> p (a d)")).then_inc(S["g_in"], 16)

            with sp.Fori(0, DEPTH) as l:
                wait(sp, "layer_done", l + 1)
                park()
                sp.dma_start(lam_raw[:, :, :], io["lam"][bass.ds(l, 1)].partition_broadcast(P)
                             .rearrange("p a b c -> p (a b) c")).then_inc(S["small_in"], 16)
                sp.dma_start(g_sub[:, :], io["g_sub"][bass.ds(l, 1), :].partition_broadcast(P)
                             .rearrange("p a d -> p (a d)")).then_inc(S["small_in"], 16)
                sp.dma_start(gate_b[:, :], io["gate_b"][bass.ds(l, 1)]
                             .rearrange("a p m -> p (a m)")).then_inc(S["small_in"], 16)
                load_g(l, 0)
                wait(sp, "zeros_done", l + 1)
                park()
                load_mod(l, 0, 2)
                load_mod(l, 2, MOD_BLOCKS // 2)
                with sp.Fori(0, TURNS) as t:
                    for g in range(6):
                        sp.wait_ge(proj[g], l * TURNS + t + 1)
                        park()
                        sp.dma_start(w_qkv[:, g], io["w_qkv"][bass.ds((l * TURNS + t) * 6 + g, 1)]
                                     .rearrange("a p k n -> p (a k) n")).then_inc(w_in[g], 16)
                wait(sp, "yd_ev", TURNS * l + TURNS + 1)
                park()
                load_g(l, 1)
                with sp.Fori(0, MT // 2) as m2:
                    for s in range(2):
                        sp.wait_ge(m_mm[s], 4 * (l * (MT // 2) + m2) + 4)
                        park()
                        sp.dma_start(w_m[:, s], io["w_m"][bass.ds(l * MT + m2 * 2 + s, 1)]
                                     .rearrange("a p k n -> p (a k) n")).then_inc(m_in[s], 16)
                        if s == 0:
                            sp.dma_start(w_out[:, bass.ds(m2 * 2, 2), :], io["w_out"][bass.ds(l, 1), :, bass.ds(m2 * 2, 2)]
                                         .rearrange("a p k n -> p (a k) n")).then_inc(S["wout_in"], 16)
                for s in range(2):
                    sp.wait_ge(m_mm[s], 4 * (MT // 2) * l + 4 * (MT // 2) + 4)
                    park()
                with sp.Fori(0, HEADS) as hq:
                    for c in range(2):
                        wait(sp, "sc_done", l * 2 * HEADS + hq * 2 + c + 1)
                        park()
                        sp.dma_start(q_w[:, c], io["w_q"][bass.ds((l * HEADS + hq) * 2 + c, 1)]
                                     .rearrange("a p k n -> p (a k) n")).then_inc(q_in[c], 16)
            wait(sp, "layer_done", DEPTH + 1)
            park()
            sp.dma_start(g_row[:, :], io["final_g"].partition_broadcast(P)).then_inc(S["g_in"], 16)
            for ch in range(CH):
                wait(sp, "out_ready", ch + 1)
                park()
                sp.dma_start(out.rearrange("b (c p) d -> p (b c) d", p=P)[:, ch, :],
                             (h_row, h_tmp)[ch % 2][:, :]).then_inc(out_done[ch % 2], 16)
            for s in range(2):
                sp.wait_ge(out_done[s], 16 * CH // 2)

        @block.tensor
        def _(pe):
            def park():
                pe.sem_inc(S["parked_pe"], 1)

            for g in range(6):
                pe.sem_inc(proj[g], 1)
            for s in range(2):
                pe.sem_inc(m_mm[s], 4)
            pe.sem_inc(S["pv_done"], 2)
            pe.sem_inc(S["y_done"], 2)
            pe.sem_inc(S["sc_done"], 2)
            pe.sem_inc(S["v_pe"], 1)
            wait(pe, "const_in", 5 * 16)
            wait(pe, "c_act_done", 1)

            def mod_rows(l, lo, hi):
                with pe.Fori(lo, hi) as n2:
                    for s in range(2):
                        n = l * MOD_BLOCKS + n2 * 2 + s
                        pe.wait_ge(ada_in[s], 32 * (l * (MOD_BLOCKS // 2) + n2) + 32)
                        wait(pe, "mod_evac", n + 1)
                        for k in range(4):
                            pe.matmul(ps[:, 6 + s, :], c_rep[:, k, :], ada_w[:, s, k, :], start=(k == 0), stop=False)
                        wait(pe, "acc_ready", n + 1)
                        pe.matmul(ps[:, 6 + s, :], ones[:, :], mod_acc[:, s, :],
                                  start=False, stop=True).then_inc(S["mod_mm"], 1)

            def norm(l, which):
                with pe.Fori(0, CH) as ch:
                    n = l * 2 * CH + which * CH + ch
                    wait(pe, "norm_h", n + 2)
                    wait(pe, "hT_ev", 2 * n + 2)
                    for half in range(2):
                        for k in range(4):
                            kk = 4 * half + k
                            last = pe.transpose(ps[:, half, k * P:(k + 1) * P], h_row[:, kk * P:(kk + 1) * P], C(IDENT))
                        last.then_inc(S["tr_done"], 1)

            def project(i, g, bank):
                pe.wait_ge(w_in[g], 16 * i + 16)
                for k in range(KD):
                    last = pe.matmul(ps[:, bank, :], w_qkv[:, g, k, :], hT[:, k, :], start=(k == 0), stop=(k == KD - 1))
                last.then_inc(proj[g], 1)

            def project_v(g, bank, chunks):
                for c in chunks:
                    for k in range(KD):
                        last = pe.matmul(ps[:, bank, c * P:(c + 1) * P], hT[:, k, c * P:(c + 1) * P],
                                         w_qkv[:, g, k, :], start=(k == 0), stop=(k == KD - 1))
                return last

            def mix(i):
                wait(pe, "dq_ready", i + 1)
                project(i, 0, 0)
                wait(pe, "dk_ready", i + 1)
                project(i, 1, 1)
                pe.wait_ge(w_in[2], 16 * i + 16)
                wait(pe, "yd_ev", i + 1)
                project_v(2, 7, range(CH)).then_inc(proj[2], 1)

                def piece(u):
                    if u == 0:
                        wait(pe, "q_ev", i + 1)
                        project(i, 3, 0)
                    if u == 2:
                        wait(pe, "k_ev", i + 1)
                        project(i, 4, 1)
                    if u == 4:
                        pe.wait_ge(w_in[5], 16 * i + 16)
                        wait(pe, "v_ev", i + 1)
                    if 4 <= u < 8:
                        last = project_v(5, 7, [u - 4])
                        if u == 7:
                            last.then_inc(proj[5], 1)
                    if u == 5:
                        wait(pe, "dqraw_ev", i + 1)
                        pe.matmul(ps[:, 0, :], C(ROPE_PERM), dq_raw, start=True, stop=True).then_inc(S["rope_mm"], 1)
                    if u == 6:
                        wait(pe, "dkraw_ev", i + 1)
                        pe.matmul(ps[:, 1, :], C(ROPE_PERM), dk_raw, start=True, stop=True).then_inc(S["rope_mm"], 1)

                def logits(u, bank, stop):
                    h, kb = u // CH, CH - 1 - u % CH
                    r = slice(HD * h, HD * h + HD)
                    return pe.matmul(ps[:, bank, 0:qcols(kb)], sb_k[r, kb * P:(kb + 1) * P], sb_q[r, kb * P:SEQ],
                                     start=True, stop=stop)

                for u in range(2 * CH + 2):
                    if u < 2 * CH:
                        if u == 0:
                            wait(pe, "q_ev", i + 1)
                            wait(pe, "k_ev", i + 1)
                        if u < 2:
                            wait(pe, "p_exp", 8 * i + 1)
                        else:
                            wait(pe, "L_done", 8 * i + u - 1)
                        logits(u, 2 + u % 2, True).then_inc(S["z_done"], 1)
                        piece(u)
                    if 1 <= u <= 2 * CH:
                        b = u - 1
                        h, kb = b // CH, CH - 1 - b % CH
                        wait(pe, "L_done", 8 * i + b + 1)
                        if b < 2:
                            wait(pe, "wt_ev", CH * i + 1)
                        else:
                            wait(pe, "w_exp", 8 * i + b - 1)
                        bank = 4 + b % 2
                        logits(b, bank, False)
                        last = pe.matmul(ps[:, bank, 0:qcols(kb)], C(NEG_UPPER), L[:, h, kb, 0:qcols(kb)],
                                         start=False, stop=(kb == CH - 1))
                        for kk in range(kb + 1, CH):
                            last = pe.matmul(ps[:, bank, (kk - kb) * P:qcols(kb)], C(NEG_ONES),
                                             L[:, h, kk, 0:qcols(kk)], start=False, stop=(kk == CH - 1))
                        last.then_inc(S["b_done"], 1)
                    if u >= 2:
                        b = u - 2
                        h, kb = b // CH, CH - 1 - b % CH
                        wait(pe, "w_masked", 8 * i + b + 1)
                        if b == 0:
                            wait(pe, "v_ev", i + 1)
                        pe.matmul(ps[HD * h:HD * h + HD, 6, kb * P:SEQ], sb_v[:, kb * P + HD * h:kb * P + HD * h + HD],
                                  w_att[:, b % 2, 0:qcols(kb)], start=(kb == CH - 1), stop=(kb == 0),
                                  skip_group_check=True).then_inc(S["pv_done"], 1)

                wait(pe, "dq_ready", i + 2)
                wait(pe, "dk_ready", i + 2)
                for step in range(CH + 3):
                    if step < CH:
                        for c in range(2):
                            v = 2 * step + c
                            if v >= 2:
                                wait(pe, "p_exp", 8 * i + v)
                            r = slice(HD * c, HD * c + HD)
                            pe.matmul(ps[:, 2 + c, 0:(step + 1) * P], dq[r, step * P:(step + 1) * P],
                                      dk[r, 0:(step + 1) * P], start=True, stop=True).then_inc(S["s_done"], 1)
                    if 1 <= step <= CH:
                        q = step - 1
                        wait(pe, "dw_done", CH * i + q + 1)
                        if q < 2:
                            wait(pe, "w_exp", 8 * i + 8)
                        else:
                            wait(pe, "wt_ev", CH * i + q)
                        for kb in range(q + 1):
                            last = pe.transpose(ps[:, 4 + q % 2, kb * P:(kb + 1) * P],
                                                prob[:, 2 * (q % 2), kb * P:(kb + 1) * P], C(IDENT))
                        last.then_inc(S["wt_done"], 1)
                    if 2 <= step <= CH + 1:
                        q = step - 2
                        wait(pe, "wt_ev", CH * i + q + 2)
                        if q == 0:
                            wait(pe, "ysb_ev", i + 1)
                            wait(pe, "dv_ev", i + 1)
                        for kb in range(q + 1):
                            last = pe.matmul(ps[:, Y_BANK[q], q * P:(q + 1) * P], w_t[:, q % 2, kb * P:(kb + 1) * P],
                                             d_v[:, kb * P:(kb + 1) * P], start=(kb == 0), stop=(kb == q))
                        last.then_inc(S["y_done"], 1)
                    if step >= 3:
                        q = step - 3
                        wait(pe, "yn_done", CH * i + q + 1)
                        pe.transpose(ps[:, 7, q * P:(q + 1) * P], y_n[:, q % 2, :], C(IDENT)).then_inc(S["yt_done"], 1)

            with pe.Fori(0, DEPTH) as l:
                mod_rows(l, 0, 2)
                norm(l, 0)
                mod_rows(l, 2, MOD_BLOCKS // 2)
                wait(pe, "hT_ev", 4 * CH * l + 2 * CH + 2)
                wait(pe, "mod_evac", MOD_BLOCKS * l + MOD_BLOCKS + 2)
                park()
                with pe.Fori(0, TURNS) as t:
                    mix(l * TURNS + t)
                wait(pe, "yd_ev", TURNS * l + TURNS + 1)
                park()
                with pe.Fori(0, MT // 2) as m2:
                    for s in range(2):
                        m = l * MT + m2 * 2 + s
                        pe.wait_ge(m_in[s], 16 * (l * (MT // 2) + m2) + 16)
                        wait(pe, "merged_done", m + 1)
                        for b, (k0, n, rhs) in enumerate(((0, KD, hT), (KD, KD, hT), (16, 4, y_sb), (20, 4, y_d))):
                            for k in range(n):
                                last = pe.matmul(ps[:, 4 * s + b, :], w_m[:, s, k0 + k, :], rhs[:, k, :],
                                                 start=(k == 0), stop=(k == n - 1))
                            last.then_inc(m_mm[s], 1)
                wait(pe, "merged_done", MT * l + MT + 2)
                wait(pe, "wout_in", 64 * l + 64)
                for c in range(CH):
                    for n in range(2):
                        for k in range(KD):
                            last = pe.matmul(ps[:, 2 * c + n, :], merged[:, k, c * P:(c + 1) * P],
                                             w_out[:, k, n * 512:(n + 1) * 512], start=(k == 0), stop=(k == KD - 1))
                        last.then_inc(S["wo_done"], 1)
                norm(l, 1)
                wait(pe, "hT_ev", 4 * CH * l + 4 * CH + 2)
                park()
                with pe.Fori(0, HEADS) as hq:
                    for c in range(2):
                        n = l * 2 * HEADS + hq * 2 + c
                        pe.wait_ge(q_in[c], 16 * (l * HEADS + hq) + 16)
                        wait(pe, "qst_ev", n + 1)
                        for k in range(KD):
                            last = pe.matmul(ps[:, c, :], q_w[:, c, k, :], hT[:, k, :], start=(k == 0), stop=(k == KD - 1))
                        last.then_inc(S["query_done"], 1)
                    for c in range(2):
                        n = l * 2 * HEADS + hq * 2 + c
                        wait(pe, "qst_ev", n + 3)
                        wait(pe, "sc_ev", n + 1)
                        for ch in range(CH):
                            last = pe.matmul(ps[:, 2 + c, ch * P:(ch + 1) * P], q_st[:, c, ch * P:(ch + 1) * P],
                                             q_w[:, c, KD, :], start=True, stop=True)
                        last.then_inc(S["sc_done"], 1)
                with pe.Fori(0, CH * HEADS) as j:
                    J = l * CH * HEADS + j
                    wait(pe, "v_added", J + 1)
                    wait(pe, "diag_done", 8 * J + 8)
                    for k in range(V_PE):
                        pe.wait_ge(v_in[k], 32 * J + 16)
                        for n in range(2):
                            last = pe.matmul(ps[:, n, :], diag[:, k, :], ring_v[:, k, n * 512:(n + 1) * 512],
                                             start=(k == 0), stop=(k == V_PE - 1))
                        last.then_inc(S["v_pe"], 1)

        @block.scalar
        def _(act):
            def park():
                act.sem_inc(S["parked_act"], 1)

            def start_root(dst, total, n):
                act.drain()
                act.activation(dst, total, ACT.Ln, scale=1.0 / n, bias=eps[:, :])
                act.drain()
                return act.activation(dst, dst, ACT.Exp, scale=-0.5)

            act.sem_inc(S["mod_evac"], 2)
            act.sem_inc(S["hT_ev"], 2)
            act.sem_inc(S["p_exp"], 1)
            act.sem_inc(S["wt_ev"], 1)
            act.sem_inc(S["yd_ev"], 1)
            act.sem_inc(S["qst_ev"], 2)
            wait(act, "const_in", 5 * 16)
            act.activation(c_sig[:, :], c_raw[:, :], ACT.Sigmoid).then_inc(S["c_sig_done"], 1)

            def mod_rows(l, lo, hi):
                with act.Fori(lo, hi) as n2:
                    for s in range(2):
                        n = l * MOD_BLOCKS + n2 * 2 + s
                        wait(act, "mod_mm", n + 1)
                        park()
                        act.copy(mod[:, :, :].rearrange("p a d -> p (a d)")[:, bass.ds((n2 * 2 + s) * 512, 512)],
                                 ps[:, 6 + s, :]).then_inc(S["mod_evac"], 1)

            def norm(l, which):
                act.preload_act_table_set("natural_log_exp_and_others")
                with act.Fori(0, CH) as ch:
                    n = l * 2 * CH + which * CH + ch
                    wait(act, "norm_h", n + 1)
                    park()
                    act.activation(junk, x[:, bass.ds(ch, 1), :].rearrange("p a d -> p (a d)"), ACT.Square,
                                   accum_out=ss[:, :])
                    start_root(root0[:, :], ss[:, :], D).then_inc(S["sq_done"], 1)
                    for half in range(2):
                        wait(act, "tr_done", 2 * n + half + 1)
                        park()
                        act.copy(hT[:, 4 * half:4 * half + 4, bass.ds(ch * P, P)],
                                 ps[:, half, :].rearrange("p (k n) -> p k n", k=4)).then_inc(S["hT_ev"], 1)

            def mix(i, t):
                act.wait_ge(proj[0], i + 2)
                act.mul(sb_q, ps[:, 0, :], SCALE).then_inc(S["q_ev"], 1)
                act.wait_ge(proj[2], i + 2)
                act.copy(sb_v, ps[:, 7, :]).then_inc(S["v_ev"], 1)
                for u in range(2 * CH + 1):
                    if u < 2 * CH:
                        n = qcols(CH - 1 - u % CH)
                        wait(act, "z_done", 8 * i + u + 1)
                        if u >= 2:
                            wait(act, "L_done", 8 * i + u - 1)
                        act.activation(soft[:, u % 2, 0:n], ps[:, 2 + u % 2, 0:n], ACT.Abs)
                        act.drain()
                        act.activation(soft[:, u % 2, 0:n], soft[:, u % 2, 0:n], ACT.Exp, scale=-1.0)
                        act.drain()
                        act.activation(soft[:, u % 2, 0:n], soft[:, u % 2, 0:n], ACT.Ln, bias=1.0).then_inc(S["ln_done"], 1)
                    if u == 2:
                        act.wait_ge(proj[3], i + 2)
                        act.mul(dq_raw, ps[:, 0, :], SCALE).then_inc(S["dqraw_ev"], 1)
                    if u == 4:
                        act.wait_ge(proj[4], i + 2)
                        act.copy(dk_raw, ps[:, 1, :]).then_inc(S["dkraw_ev"], 1)
                    if u >= 1:
                        b = u - 1
                        n = qcols(CH - 1 - b % CH)
                        wait(act, "b_done", 8 * i + b + 1)
                        wait(act, "pv_done", 8 * i + b + 1)
                        act.activation(w_att[:, b % 2, 0:n], ps[:, 4 + b % 2, 0:n], ACT.Exp).then_inc(S["w_exp"], 1)
                act.wait_ge(proj[5], i + 2)
                act.copy(d_v, ps[:, 7, :]).then_inc(S["dv_ev"], 1)
                for step in range(CH + 2):
                    if step < CH:
                        for c in range(2):
                            v = 2 * step + c
                            n = (step + 1) * P
                            wait(act, "max_done", 8 * i + v + 1)
                            if step >= 2:
                                wait(act, "wt_done", CH * i + step - 1)
                            act.activation(prob[:, 2 * (step % 2) + c, 0:n], ps[:, 2 + c, 0:n], ACT.Exp,
                                           bias=nmax[:, v:v + 1], accum_out=zsum[:, v:v + 1]).then_inc(S["p_exp"], 1)
                    if 1 <= step <= CH:
                        q = step - 1
                        wait(act, "wt_done", CH * i + q + 1)
                        wait(act, "y_done", CH * i + q + 1)
                        act.copy(w_t[:, q % 2, 0:(q + 1) * P], ps[:, 4 + q % 2, 0:(q + 1) * P]).then_inc(S["wt_ev"], 1)
                    if step >= 2:
                        q = step - 2
                        wait(act, "y_done", CH * i + q + 3)
                        act.activation(junk_y, ps[:, Y_BANK[q], q * P:(q + 1) * P], ACT.Square,
                                       accum_out=yss[:, q:q + 1])
                        start_root(yroot0[:, q:q + 1], yss[:, q:q + 1], P).then_inc(S["y_sq"], 1)
                wait(act, "yt_done", CH * i + CH)
                park()
                act.copy(y_d[:, bass.ds(t, 1), :].rearrange("p a n -> p (a n)"), ps[:, 7, :]).then_inc(S["yd_ev"], 1)

            with act.Fori(0, DEPTH) as l:
                mod_rows(l, 0, 2)
                wait(act, "x_in", 16)
                wait(act, "lam_summed", l + 1)
                act.activation(lam_exp[:, :], lam_sum[:, :], ACT.Exp).then_inc(S["lam_exped"], 1)
                norm(l, 0)
                mod_rows(l, 2, MOD_BLOCKS // 2)
                act.preload_act_table_set("natural_log_exp_and_others")
                with act.Fori(0, TURNS) as t:
                    mix(l * TURNS + t, t)
                with act.Fori(0, MT // 2) as m2:
                    for s in range(2):
                        m = l * MT + m2 * 2 + s
                        wait(act, "merged_done", m + 1)
                        for b in range(2):
                            act.wait_ge(m_mm[s], 4 * (l * (MT // 2) + m2) + b + 5)
                            park()
                            act.activation(sig[:, s, b, :], ps[:, 4 * s + b, :], ACT.Sigmoid,
                                           bias=gate_b[:, bass.ds(b * MT + m2 * 2 + s, 1)]).then_inc(S["sig_done"], 1)
                wait(act, "x_upd", 2 * CH * l + 2 * CH)
                park()
                norm(l, 1)
                with act.Fori(0, HEADS) as hq:
                    for c in range(2):
                        n = l * 2 * HEADS + hq * 2 + c
                        wait(act, "query_done", n + 1)
                        wait(act, "sc_done", n + 1)
                        act.copy(q_st[:, c, :], ps[:, c, :]).then_inc(S["qst_ev"], 1)
                with act.Fori(0, CH * HEADS) as j:
                    J = l * CH * HEADS + j
                    wait(act, "topk_done", J + l + 1)
                    act.activation(gexp, best, ACT.Exp, bias=nbest, accum_out=gsum).then_inc(S["gate_exp"], 1)
                    wait(act, "dots_done", J + 1)
                    act.activation(gel, dots, ACT.Gelu).then_inc(S["gelu_done"], 1)
                    wait(act, "coef_done", J + 1)
                    wait(act, "v_pe", 8 * J + 1)
                    for k in range(V_PE):
                        act.activation(diag[:, k, :], C(IDENT), ACT.Copy, scale=coef[:, k:k + 1]).then_inc(S["diag_done"], 1)
            act.preload_act_table_set("natural_log_exp_and_others")
            wait(act, "layer_done", DEPTH + 1)
            for ch in range(CH):
                if ch:
                    wait(act, "out_ready", ch)
                act.activation(junk, x[:, ch, :], ACT.Square, accum_out=ss[:, :])
                start_root(root0[:, :], ss[:, :], D).then_inc(S["out_sq"], 1)

        @block.gpsimd
        def _(pool):
            def park():
                pool.sem_inc(S["parked_pool"], 1)

            with pool.Fori(0, DEPTH) as l:
                with pool.Fori(0, TURNS) as t:
                    i = l * TURNS + t
                    for u in range(2 * CH):
                        wait(pool, "w_exp", 8 * i + u + 1)
                        park()
                        pool.affine_select(out=w_att[:, u % 2, 0:P], in_=w_att[:, u % 2, 0:P], compare_op=ALU.is_gt,
                                           fill=0.0, base=0, pattern=[[1, P]], channel_multiplier=-1
                                           ).then_inc(S["w_masked"], 1)
                with pool.Fori(0, CH * HEADS) as j:
                    J = l * CH * HEADS + j
                    wait(pool, "topk_done", J + l + 1)
                    wait(pool, "u_used", 2 * RING * J + RING)
                    park()
                    pool.tensor_copy(idx_u[:, :], idx_next[:, :]).then_inc(S["idx_u_set"], 1)
                    wait(pool, "idx_u_set", J + 1)
                    for k in range(TOPK):
                        wait(pool, "u_used", TOPK * J + k + 1)
                        park()
                        pool.indirect_dma_start(out=ring_u[:, k % RING, :], out_offset=None, in_=io["u"],
                                                in_offset=bass.IndirectOffsetOnAxis(ap=idx_u[:, k:k + 1], axis=0)
                                                ).then_inc(u_in[k % RING], 16)
                    wait(pool, "v_dve", RING * J + RING)
                    park()
                    pool.tensor_copy(idx_v[:, :], idx_next[:, :]).then_inc(S["idx_taken"], 1)
                    wait(pool, "idx_taken", J + 1)
                    for k in range(TOPK):
                        if k < RING:
                            wait(pool, "v_dve", RING * J + k + 1)
                        else:
                            wait(pool, "v_pe", RING * J + k - RING + 2)
                        park()
                        pool.indirect_dma_start(out=ring_v[:, k % RING, :], out_offset=None, in_=io["v"],
                                                in_offset=bass.IndirectOffsetOnAxis(ap=idx_v[:, k:k + 1], axis=0)
                                                ).then_inc(v_in[k % RING], 16)

        @block.vector
        def _(dve):
            def park():
                dve.sem_inc(S["parked_dve"], 1)

            dve.memset(ones[:, :], 1.0)
            dve.memset(eps[:, :], EPS)
            for i in range(DEPTH):
                dve.memset(lam_init[:, i:i + 1], LAM_INIT[i])
                dve.memset(lam_rest[:, i:i + 1], 1.0 - LAM_INIT[i])
                dve.memset(expert0[:, i:i + 1], float(i * N_EXPERTS))
            for name, n in (("layer_done", 1), ("norm_gain", 1), ("norm_h", 1), ("dq_ready", 1), ("dk_ready", 1),
                            ("merged_done", 2), ("sc_ev", 2), ("v_added", 1), ("u_used", RING), ("v_dve", RING)):
                dve.sem_inc(S[name], n)
            wait(dve, "c_sig_done", 1)
            dve.tensor_tensor(c_act[:, :], c_sig[:, :], c_raw[:, :], ALU.mult)
            dve.drain()
            for k in range(KD):
                last = dve.tensor_scalar(c_rep[:, k, :], ones[:, :], c_act[:, k:k + 1], None, ALU.mult)
            last.then_inc(S["c_act_done"], 1)

            def mod_rows(l, lo, hi):
                with dve.Fori(lo, hi) as n2:
                    for s in range(2):
                        n = l * MOD_BLOCKS + n2 * 2 + s
                        dve.wait_ge(ada_in[s], 32 * (l * (MOD_BLOCKS // 2) + n2) + 32)
                        wait(dve, "mod_evac", n + 1)
                        dve.scalar_tensor_tensor(mod_acc[:, s, :], ada_w[:, s, 4, :], c_act[:, 4:5], bias0[:, s, :],
                                                 ALU.mult, ALU.add)
                        for k in range(5, KD):
                            dve.drain()
                            last = dve.scalar_tensor_tensor(mod_acc[:, s, :], ada_w[:, s, k, :], c_act[:, k:k + 1],
                                                            mod_acc[:, s, :], ALU.mult, ALU.add)
                        last.then_inc(S["acc_ready"], 1)

            def inv_root_mean(dst, start, total, n):
                dve.tensor_scalar(newton[:, 0:1], total, 1.0 / n, EPS, ALU.mult, ALU.add)
                dve.tensor_tensor(newton[:, 1:2], start, start, ALU.mult)
                dve.drain()
                dve.tensor_tensor(newton[:, 0:1], newton[:, 0:1], newton[:, 1:2], ALU.mult)
                dve.drain()
                dve.tensor_scalar(newton[:, 0:1], newton[:, 0:1], -0.5, 1.5, ALU.mult, ALU.add)
                dve.drain()
                dve.tensor_tensor(dst, start, newton[:, 0:1], ALU.mult)
                dve.drain()

            def norm(l, which):
                shift, gain = mod[:, 3 * which, :], mod[:, 3 * which + 1, :]
                wait(dve, "g_in", 32 * l + 16 * which + 16)
                wait(dve, "mod_evac", l * MOD_BLOCKS + (MOD_BLOCKS if which else 4) + 2)
                dve.scalar_tensor_tensor(gain, gain, 1.0, g_row[:, :], ALU.add, ALU.mult).then_inc(S["norm_gain"], 1)
                dve.drain()
                with dve.Fori(0, CH) as ch:
                    n = l * 2 * CH + which * CH + ch
                    wait(dve, "sq_done", n + 1)
                    inv_root_mean(rstd[:, :], root0[:, :], ss[:, :], D)
                    dve.scalar_tensor_tensor(h_tmp[:, :], x[:, bass.ds(ch, 1), :].rearrange("p a d -> p (a d)"),
                                             rstd[:, 0:1], gain, ALU.mult, ALU.mult)
                    dve.drain()
                    if which:
                        dve.tensor_tensor(h2[:, bass.ds(ch, 1), :].rearrange("p a d -> p (a d)"), h_tmp[:, :], shift,
                                          ALU.add)
                    wait(dve, "hT_ev", 2 * n + 2)
                    dve.tensor_tensor(h_row[:, :], h_tmp[:, :], shift, ALU.add).then_inc(S["norm_h"], 1)

            def rope(i, which, raw, dst, bank, done):
                wait(dve, "dkraw_ev" if which else "dqraw_ev", i + 1)
                dve.tensor_tensor(rope_tmp[:, 0, :], raw, cos_t[:, :], ALU.mult)
                wait(dve, "rope_mm", 2 * i + which + 1)
                dve.tensor_tensor(rope_tmp[:, 1, :], ps[:, bank, :], sin_t[:, :], ALU.mult)
                dve.drain()
                dve.tensor_tensor(dst, rope_tmp[:, 0, :], rope_tmp[:, 1, :], ALU.add).then_inc(S[done], 1)
                dve.drain()

            def mix(i, t):
                dve.wait_ge(proj[1], i + 2)
                dve.tensor_copy(sb_k, ps[:, 1, :]).then_inc(S["k_ev"], 1)
                for u in range(2 * CH + 1):
                    if u >= 1:
                        b = u - 1
                        h, kb = b // CH, CH - 1 - b % CH
                        n = qcols(kb)
                        wait(dve, "ln_done", 8 * i + b + 1)
                        dve.scalar_tensor_tensor(L[:, h, kb, 0:n], ps[:, 2 + b % 2, 0:n], 0.0, soft[:, b % 2, 0:n],
                                                 ALU.max, ALU.add)
                        dve.drain()
                        dve.tensor_tensor(L[:, h, kb, 0:P], L[:, h, kb, 0:P], C(STRICT), ALU.mult).then_inc(S["L_done"], 1)
                        dve.drain()
                    if u == 6:
                        rope(i, 0, dq_raw, dq, 0, "dq_ready")
                    if u == 7:
                        rope(i, 1, dk_raw, dk, 1, "dk_ready")
                wait(dve, "pv_done", 8 * i + 8 + 2)
                dve.tensor_copy(y_sb[:, bass.ds(t, 1), :].rearrange("p a n -> p (a n)"), ps[:, 6, :]).then_inc(S["ysb_ev"], 1)
                for step in range(CH + 3):
                    if step < CH:
                        for c in range(2):
                            v = 2 * step + c
                            wait(dve, "s_done", 8 * i + v + 1)
                            dve.tensor_tensor(ps[:, 2 + c, step * P:(step + 1) * P], ps[:, 2 + c, step * P:(step + 1) * P],
                                              C(NEG_MASK), ALU.add)
                            dve.drain()
                            dve.tensor_reduce(nmax[:, v:v + 1], ps[:, 2 + c, 0:(step + 1) * P], AX.X, ALU.max,
                                              negate=True).then_inc(S["max_done"], 1)
                    if 1 <= step <= CH:
                        q = step - 1
                        n = (q + 1) * P
                        p0, p1 = prob[:, 2 * (q % 2), 0:n], prob[:, 2 * (q % 2) + 1, 0:n]
                        wait(dve, "p_exp", 8 * i + 2 * q + 3)
                        dve.reciprocal(rz[:, 2 * q:2 * q + 2], zsum[:, 2 * q:2 * q + 2])
                        dve.drain()
                        dve.tensor_scalar(p1, p1, rz[:, 2 * q + 1:2 * q + 2], neg_lam[:, 0:1], ALU.mult, ALU.mult)
                        dve.drain()
                        dve.scalar_tensor_tensor(p0, p0, rz[:, 2 * q:2 * q + 1], p1, ALU.mult, ALU.add).then_inc(S["dw_done"], 1)
                        dve.drain()
                    if step >= 3:
                        q = step - 3
                        wait(dve, "y_sq", CH * i + q + 1)
                        inv_root_mean(yr[:, q:q + 1], yroot0[:, q:q + 1], yss[:, q:q + 1], P)
                        if q >= 2:
                            wait(dve, "yt_done", CH * i + q - 1)
                        dve.scalar_tensor_tensor(y_n[:, q % 2, :], ps[:, Y_BANK[q], q * P:(q + 1) * P], yr[:, q:q + 1], g_sub[:, :],
                                                 ALU.mult, ALU.mult).then_inc(S["yn_done"], 1)

            def topk_pair(vals, idxs, src, work):
                dve.max(vals[:, 0:8], src)
                dve.drain()
                dve.max_index(idxs[:, 0:8], vals[:, 0:8], src)
                dve.match_replace(work, vals[:, 0:8], src, LOWEST)
                dve.drain()
                dve.max(vals[:, 8:16], work)
                dve.drain()
                dve.max_index(idxs[:, 8:16], vals[:, 8:16], work)

            def topk(l, at_pair, count):
                if count is not None:
                    wait(dve, "idx_taken", count)
                    wait(dve, "gate_exp", count)
                    park()
                dve.tensor_copy(sc_in, scores[:, bass.ds(at_pair, 1), :].rearrange("p a (c n) -> p (a c) n", c=2))
                dve.drain()
                for c in range(2):
                    topk_pair(s_top[:, c, :], i_top[:, c, :], sc_in[:, c, :], sc_work[:, c, :])
                dve.drain()
                dve.tensor_copy(i_top_f, i_top[:, :, :])
                dve.tensor_tensor(cand, s_top[:, 0, :].unsqueeze(2).broadcast_to([P, TOPK, TOPK]),
                                  s_top[:, 1, :].unsqueeze(1).broadcast_to([P, TOPK, TOPK]), ALU.add)
                dve.drain()
                flat = cand.rearrange("p a b -> p (a b)")
                topk_pair(best, pos[:, :], flat, cand_work.rearrange("p a b -> p (a b)"))
                dve.drain()
                dve.tensor_scalar(nbest, best[:, 0:1], -1.0, None, ALU.mult)
                dve.tensor_scalar(pos_hl[:, 0, :], pos[:, :], 4, None, ALU.logical_shift_right)
                dve.tensor_scalar(pos_hl[:, 1, :], pos[:, :], 15, None, ALU.bitwise_and)
                dve.drain()
                dve.tensor_copy(pos_f, pos_hl[:, :, :])
                dve.drain()
                for c in range(2):
                    dve.tensor_tensor(onehot, pos_f[:, c, :].unsqueeze(2).broadcast_to([P, TOPK, TOPK]),
                                      iota16[:, :].unsqueeze(1).broadcast_to([P, TOPK, TOPK]), ALU.is_equal)
                    dve.drain()
                    dve.tensor_tensor(onehot, onehot, i_top_f[:, c, :].unsqueeze(1).broadcast_to([P, TOPK, TOPK]), ALU.mult)
                    dve.drain()
                    dve.tensor_reduce(sel_f[:, c, :], onehot, AX.X, ALU.add)
                    dve.drain()
                dve.scalar_tensor_tensor(sel_f[:, 0, :], sel_f[:, 0, :], float(N_KEYS), sel_f[:, 1, :], ALU.mult, ALU.add)
                dve.drain()
                dve.tensor_scalar(idx_next[:, :], sel_f[:, 0, :], expert0[:, bass.ds(l, 1)], None,
                                  ALU.add).then_inc(S["topk_done"], 1)

            with dve.Fori(0, DEPTH) as l:
                dve.memset(bias0, 0.0).then_inc(S["zeros_done"], 1)
                wait(dve, "small_in", 48 * l + 48)
                for c in range(2):
                    dve.tensor_tensor(lam_prod[:, c, :], lam_raw[:, 2 * c, :], lam_raw[:, 2 * c + 1, :], ALU.mult)
                dve.drain()
                dve.tensor_reduce(lam_sum[:, :], lam_prod[:, :, :], AX.X, ALU.add).then_inc(S["lam_summed"], 1)
                dve.tensor_scalar(g_sub[:, :], g_sub[:, :], lam_rest[:, bass.ds(l, 1)], None, ALU.mult)
                mod_rows(l, 0, 2)
                wait(dve, "lam_exped", l + 1)
                dve.tensor_tensor(neg_lam[:, :], lam_exp[:, 1:2], lam_exp[:, 0:1], ALU.subtract)
                dve.drain()
                dve.tensor_tensor(neg_lam[:, :], neg_lam[:, :], lam_init[:, bass.ds(l, 1)], ALU.subtract)
                norm(l, 0)
                mod_rows(l, 2, MOD_BLOCKS // 2)
                wait(dve, "mod_evac", l * MOD_BLOCKS + MOD_BLOCKS + 2)
                park()
                with dve.Fori(0, TURNS) as t:
                    mix(l * TURNS + t, t)
                with dve.Fori(0, MT // 2) as m2:
                    for s in range(2):
                        m = l * MT + m2 * 2 + s
                        for b in range(2):
                            wait(dve, "sig_done", 2 * m + b + 1)
                            dve.wait_ge(m_mm[s], 4 * (l * (MT // 2) + m2) + b + 7)
                            dve.tensor_tensor(sig[:, s, b, :], sig[:, s, b, :], ps[:, 4 * s + 2 + b, :], ALU.mult)
                        dve.drain()
                        dve.tensor_tensor(merged[:, bass.ds(m2 * 2 + s, 1), :].rearrange("p a n -> p (a n)"),
                                          sig[:, s, 0, :], sig[:, s, 1, :], ALU.add).then_inc(S["merged_done"], 1)
                dve.drain()
                for c in range(CH):
                    for n in range(2):
                        cols = slice(n * 512, (n + 1) * 512)
                        wait(dve, "wo_done", 2 * CH * l + 2 * c + n + 1)
                        dve.tensor_tensor(out_tmp, ps[:, 2 * c + n, :], mod[:, 2, cols], ALU.mult)
                        dve.drain()
                        dve.tensor_tensor(x[:, c, cols], x[:, c, cols], out_tmp, ALU.add).then_inc(S["x_upd"], 1)
                        dve.drain()
                norm(l, 1)
                with dve.Fori(0, HEADS) as hq:
                    for c in range(2):
                        n = l * 2 * HEADS + hq * 2 + c
                        wait(dve, "sc_done", n + 3)
                        dve.tensor_copy(scores[:, 0:CH * HEADS, :].rearrange("p (c h) n -> p c h n", c=CH)
                                        [:, :, bass.ds(hq, 1), c * N_KEYS:(c + 1) * N_KEYS]
                                        .rearrange("p c h n -> p c (h n)"),
                                        ps[:, 2 + c, :].rearrange("p (c n) -> p c n", c=CH)).then_inc(S["sc_ev"], 1)
                dve.memset(scores[:, CH * HEADS, :], 0.0)
                dve.drain()
                topk(l, 0, None)
                with dve.Fori(0, CH) as ch:
                    dve.drain()
                    dve.tensor_copy(h_tmp[:, :], h2[:, bass.ds(ch, 1), :].rearrange("p a d -> p (a d)"))
                    dve.memset(h_row[:, :], 0.0)
                    dve.drain()
                    with dve.Fori(0, HEADS) as hd:
                        j = ch * HEADS + hd
                        J = l * CH * HEADS + j
                        for k in range(TOPK):
                            dve.wait_ge(u_in[k % RING], 32 * J + 16 * (k // RING) + 16)
                            row = ring_u[:, k % RING, :]
                            dve.tensor_tensor_reduce(row, row, h_tmp[:, :], 1.0, 0.0, ALU.mult, ALU.add,
                                                     dots[:, k:k + 1]).then_inc(S["u_used"], 1)
                        dve.drain().then_inc(S["dots_done"], 1)
                        wait(dve, "gate_exp", J + 1)
                        dve.reciprocal(rsum, gsum)
                        dve.drain()
                        wait(dve, "gelu_done", J + 1)
                        dve.scalar_tensor_tensor(coef, gel, rsum, gexp, ALU.mult, ALU.mult).then_inc(S["coef_done"], 1)
                        topk(l, j + 1, J + 1)
                        for k in range(V_PE, TOPK):
                            dve.wait_ge(v_in[k % RING], 32 * J + 32)
                            dve.scalar_tensor_tensor(h_row[:, :], ring_v[:, k % RING, :], coef[:, k:k + 1], h_row[:, :],
                                                     ALU.mult, ALU.add).then_inc(S["v_dve"], 1)
                            dve.drain()
                        wait(dve, "v_pe", 8 * J + 8 + 1)
                        dve.tensor_tensor(h_row[:, :], h_row[:, :], ps[:, 0:2, :].rearrange("p a n -> p (a n)"),
                                          ALU.add).then_inc(S["v_added"], 1)
                        dve.drain()
                    dve.tensor_tensor(h_row[:, :], h_row[:, :], mod[:, 5, :], ALU.mult)
                    dve.drain()
                    xc = x[:, bass.ds(ch, 1), :].rearrange("p a d -> p (a d)")
                    dve.tensor_tensor(xc, xc, h_row[:, :], ALU.add)
                dve.drain().then_inc(S["layer_done"], 1)

            wait(dve, "g_in", 32 * DEPTH + 16)
            for ch in range(CH):
                wait(dve, "out_sq", ch + 1)
                inv_root_mean(rstd[:, :], root0[:, :], ss[:, :], D)
                if ch >= 2:
                    dve.wait_ge(out_done[ch % 2], 16 * (ch // 2))
                dve.scalar_tensor_tensor((h_row, h_tmp)[ch % 2][:, :], x[:, ch, :], rstd[:, 0:1], g_row[:, :],
                                         ALU.mult, ALU.mult).then_inc(S["out_ready"], 1)
                dve.drain()


def shape_constants():
    i, j = np.arange(P)[:, None], np.arange(P)[None, :]
    const = np.zeros((P, N_CONST, P), np.float32)
    const[:, IDENT] = i == j
    const[:, NEG_UPPER] = -1.0 * (i >= j)
    const[:, NEG_ONES] = -1.0
    const[:, STRICT] = i < j
    const[:, NEG_MASK] = -1e30 * (j > i)
    half = ROT // 2
    in_head = j % HD
    const[:, ROPE_PERM] = (1.0 * ((in_head >= half) & (in_head < ROT) & (i == j - half))
                           - 1.0 * ((in_head < half) & (i == j + half)))
    inv_freq = (1.0 / (np.float32(ROPE_THETA) ** (np.arange(0, ROT, 2, dtype=np.float32) / np.float32(ROT))))
    angle = inv_freq.astype(np.float32)[:, None] * np.arange(SEQ, dtype=np.float32)[None, :]
    cos_t, sin_t = np.ones((P, SEQ), np.float32), np.zeros((P, SEQ), np.float32)
    for p in range(P):
        if p % HD < ROT:
            cos_t[p], sin_t[p] = np.cos(angle[p % half]), np.sin(angle[p % half])
    return {"const": const, "cos": cos_t, "sin": sin_t, "iota16": np.arange(TOPK, dtype=np.float32)}


def lay_out(a):
    L = DEPTH
    w_in = a["w_in"].reshape(L, KD, P, -1)
    groups = w_in[..., :6 * 512].reshape(L, KD, P, 6, TURNS, P)
    gates = w_in[..., 6 * 512:].reshape(L, KD, P, 2, MT, P)
    b_sb = a["w_branch_sb"].reshape(L, 4, P, MT, P)
    b_d = a["w_branch_diff"].reshape(L, 4, P, MT, P)
    w_m = np.concatenate([gates[:, :, :, 0], gates[:, :, :, 1], b_sb, b_d], axis=1)
    wq = a["peer_wq"].reshape(L, KD, P, 2 * HEADS, P).transpose(0, 3, 2, 1, 4)
    sub = a["peer_subkeys"].reshape(L, 2 * HEADS, N_KEYS, P).transpose(0, 1, 3, 2)[:, :, :, None, :]
    return {
        "x": a["x"][0],
        "c": a["c"].reshape(KD, P).T,
        "norm_g": np.stack([a["norm1_g"], a["norm2_g"]], axis=1).reshape(2 * L, D),
        "ada_w": a["ada_w"].reshape(L, KD, P, MOD_BLOCKS, 512).transpose(0, 3, 2, 1, 4).reshape(-1, P, KD, 512),
        "ada_b": a["ada_b"].reshape(L * MOD_BLOCKS, 512),
        "w_qkv": groups.transpose(0, 4, 3, 2, 1, 5).reshape(-1, P, KD, P),
        "w_m": w_m.transpose(0, 3, 2, 1, 4).reshape(-1, P, 24, P),
        "w_out": a["w_out"].reshape(L, KD, P, D).transpose(0, 2, 1, 3),
        "w_q": np.concatenate([wq, sub], axis=3).reshape(-1, P, KD + 1, P),
        "gate_b": a["gate_b"].reshape(L, 2 * MT, P).transpose(0, 2, 1),
        "lam": a["diff_lambda"],
        "g_sub": a["diff_subln_g"],
        "u": a["peer_u"].reshape(L * N_EXPERTS, D),
        "v": a["peer_v"].reshape(L * N_EXPERTS, D),
        "final_g": a["final_g"],
    }


def kernel(**inputs):
    import concourse.bacc as bacc
    from concourse.bass_utils import run_bass_kernel_spmd

    laid = lay_out({n: np.asarray(v) for n, v in inputs.items()})
    laid.update(shape_constants())
    nc = bacc.Bacc("TRN2", target_bir_lowering=False, num_devices=1)
    arrays, io = {}, {}
    for name, a in laid.items():
        a = np.ascontiguousarray(a)
        arrays[f"in_{name}_dram"] = a
        io[name] = nc.dram_tensor(f"in_{name}_dram", a.shape, mybir.dt.from_np(a.dtype), kind="ExternalInput").ap()
    out = nc.dram_tensor("out_dram", (1, SEQ, D), F32, kind="ExternalOutput").ap()
    build(nc, io, out)
    r = run_bass_kernel_spmd(nc, [arrays], core_ids=[0])
    return r.results[0]["out_dram"]
```

```python
import math
from contextlib import ExitStack

import numpy as np

import concourse.bass as bass
from concourse import mybir

F32 = mybir.dt.float32
U32 = mybir.dt.uint32
ALU = mybir.AluOpType
ACT = mybir.ActivationFunctionType
AX = mybir.AxisListType

P = 128
D = 1024
KD = D // P
SEQ = 512
CH = SEQ // P
DEPTH = 2
HD = 64
TURNS = 4
MT = D // P
N_KEYS = 128
N_EXPERTS = N_KEYS * N_KEYS
HEADS = 8
TOPK = 16
EPS = 1e-6
ROT = 16
ROPE_THETA = 500000.0
SCALE = 1.0 / math.sqrt(HD)
MOD_BLOCKS = 6 * D // 512
FIRST_BLOCKS = 4
TURN_BLOCKS = MOD_BLOCKS // TURNS
GATE1, SHIFT2, GAIN2, GATE2, SHIFT1, GAIN1 = range(6)
RING = 8
V_PE = 8
LOWEST = -3.0e38
LAM_INIT = [0.8 - 0.6 * math.exp(-0.3 * i) for i in range(DEPTH)]
IDENT, NEG_UPPER, NEG_ONES, STRICT, NEG_MASK, ROPE_PERM = range(6)
N_CONST = 6
Y_BANK = [6, 0, 1, 6]

A_WQKV = 0
A_SOFT = 6144
A_W = 7168
A_QKV = 8192
A_L = 12288
A_P = 16384
A_WT = 18432
A_YN = 19456
A_ROPE = 19712
A_YSB = 20736
A_YD = 22784
A_MERGED = 24832
A_SIG = 28928
A_WOUT = 8192
A_MW = 0
A_ADAW = 24832
A_ACC = 28928
A_BIAS = 30464
A_RING = 0
A_QW = 24832
A_QST = 27136
A_PEER_SUM = 20736
A_TOPK = 16384
A_SCORES = 19712
A_H2 = 28160
ARENA = 32256


def build(nc, io, out):
    with ExitStack() as ctx:
        def sb(name, shape, dt=F32):
            return ctx.enter_context(nc.sbuf_tensor(name, shape, dt))

        def sem(name):
            return ctx.enter_context(nc.semaphore(name))

        ps = ctx.enter_context(nc.psum_tensor("ps", [P, 8, 512], F32))
        x = sb("x_res", [P, CH, D])
        hT = sb("hT", [P, KD, SEQ])
        mod = sb("mod", [P, 6, D])
        g_row = sb("g_row", [P, D])
        h_tmp = sb("h_tmp", [P, D])
        h_row = sb("h_row", [P, D])
        const = sb("const", [P, N_CONST, P])
        ones = sb("ones", [P, P])
        cos_t = sb("cos_t", [P, SEQ])
        sin_t = sb("sin_t", [P, SEQ])
        c_raw = sb("c_raw", [P, KD])
        c_sig = sb("c_sig", [P, KD])
        c_act = sb("c_act", [P, KD])
        lam_sum = sb("lam_sum", [P, 2])
        lam_exp = sb("lam_exp", [P, 2])
        lam_init = sb("lam_init", [P, DEPTH])
        lam_rest = sb("lam_rest", [P, DEPTH])
        neg_lam = sb("neg_lam", [P, 1])
        g_sub = sb("g_sub", [P, P])
        gate_b = sb("gate_b", [P, 2 * MT])
        ss = sb("ss", [P, CH])
        root0 = sb("root0", [P, CH])
        rstd = sb("rstd", [P, CH])
        newton = sb("newton", [P, 2, CH])
        eps = sb("eps", [P, 1])
        nmax = sb("nmax", [P, 8])
        zsum = sb("zsum", [P, 8])
        rz = sb("rz", [P, 8])
        yss = sb("yss", [P, CH])
        yroot0 = sb("yroot0", [P, CH])
        yr = sb("yr", [P, CH])
        arena = sb("arena", [P, ARENA])

        def part(at, *dims):
            n = int(np.prod(dims))
            v = arena[:, at:at + n]
            if len(dims) == 2:
                v = v.rearrange("p (a b) -> p a b", a=dims[0])
            if len(dims) == 3:
                v = v.rearrange("p (a b c) -> p a b c", a=dims[0], b=dims[1])
            return v

        w_qkv = part(A_WQKV, 6, KD, P)
        soft = part(A_SOFT, 2, SEQ)
        junk_y = part(A_SOFT, P)
        lam_raw = part(A_W, 4, HD)
        lam_prod = part(A_W + 4 * HD, 2, HD)
        w_att = part(A_W, 2, SEQ)
        qkv = part(A_QKV, 8, SEQ)
        sb_q, sb_k, sb_v, dq_raw, dk_raw, dq, dk, d_v = (qkv[:, n, :] for n in range(8))
        L = part(A_L, 2, CH, SEQ)
        prob = part(A_P, 4, SEQ)
        w_t = part(A_WT, 2, SEQ)
        y_n = part(A_YN, 2, P)
        rope_tmp = part(A_ROPE, 2, SEQ)
        y_sb = part(A_YSB, TURNS, SEQ)
        y_d = part(A_YD, TURNS, SEQ)
        merged = part(A_MERGED, MT, SEQ)
        sig = part(A_SIG, 2, 2, SEQ)
        w_out = part(A_WOUT, KD, D)
        w_m = part(A_MW, 2, 24, P)
        ada_w = part(A_ADAW, 2, KD, 256)
        mod_acc = part(A_ACC, TURN_BLOCKS, 512)
        bias0 = part(A_BIAS, TURN_BLOCKS, 512)
        bias_first = part(A_QKV, FIRST_BLOCKS, 512)
        h1 = part(A_L, CH, D)
        out_tmp = part(A_SIG, 512)
        q_w = part(A_QW, 2, KD + 1, P)
        q_st = part(A_QST, 2, SEQ)
        ring_u = part(A_RING, RING, D)
        ring_v = part(A_RING + RING * D, RING, D)
        scores = part(A_SCORES, CH, 2, N_KEYS)
        peer_sum = part(A_PEER_SUM, CH, D)
        h2 = part(A_H2, CH, D)
        at = [A_TOPK]

        def small(*dims):
            v = part(at[0], *dims)
            at[0] += int(np.prod(dims))
            assert at[0] <= A_SCORES
            return v

        sc_work = small(2, N_KEYS)
        cand = small(TOPK, TOPK)
        cand_work = small(TOPK, TOPK)
        onehot = small(TOPK, TOPK)
        s_top = small(2, TOPK)
        i_top_f = small(2, TOPK)
        best = small(TOPK)
        pos_f = small(2, TOPK)
        sel_f = small(2, TOPK)
        gexp = small(TOPK)
        gsum = small(1)
        rsum = small(1)
        nbest = small(1)
        dots = small(TOPK)
        gel = small(TOPK)
        coef = small(TOPK)
        diag = small(V_PE, P)
        i_top = sb("i_top", [P, 2, TOPK], U32)
        pos = sb("pos", [P, TOPK], U32)
        pos_hl = sb("pos_hl", [P, 2, TOPK], U32)
        idx_next = sb("idx_next", [P, TOPK], U32)
        idx_u = sb("idx_u", [P, TOPK], U32)
        idx_v = sb("idx_v", [P, TOPK], U32)
        iota16 = sb("iota16", [P, TOPK])
        expert0 = sb("expert0", [P, DEPTH])

        S = {n: sem(n) for n in (
            "const_in x_in c_sig_done c_act_done zeros_done layer_done small_in lam_summed lam_exped g_in "
            "norm_gain bias_in mod_mm mod_evac acc_done sq_done norm_h tr_done hT_ev "
            "q_ev k_ev v_ev dqraw_ev dkraw_ev dv_ev rope_mm dq_ready dk_ready "
            "z_done  ln_done L_done b_done w_exp w_masked pv_done ysb_ev "
            "s_done max_done p_exp dw_done wt_done wt_ev y_done y_sq yn_done yt_done yd_ev "
            "sig_done merged_done wout_in wo_done x_upd "
            "query_done qst_ev sc_done sc_ev topk_done idx_taken gate_exp dots_done gelu_done coef_done diag_done "
            "idx_u_set u_used v_dve v_pe v_added out_sq out_ready out_done "
            "parked_act parked_dve parked_pool parked_pe parked_sp").split()}
        ada_in = [sem(f"ada_in{i}") for i in range(2)]
        w_in = [sem(f"w_in{i}") for i in range(6)]
        proj = [sem(f"proj{i}") for i in range(6)]
        m_in = [sem(f"m_in{i}") for i in range(2)]
        m_mm = [sem(f"m_mm{i}") for i in range(2)]
        q_in = [sem(f"q_in{i}") for i in range(2)]
        u_in = [sem(f"u_in{i}") for i in range(RING)]
        v_in = [sem(f"v_in{i}") for i in range(RING)]

        def C(n):
            return const[:, n, :]

        def qcols(kb):
            return SEQ - P * kb

        block = ctx.enter_context(nc.Block())

        @block.sync
        def _(sp):
            def park():
                sp.sem_inc(S["parked_sp"], 1)

            sp.dma_start(c_raw[:, :], io["c"]).then_inc(S["const_in"], 16)
            sp.dma_start(const[:, :, :], io["const"]).then_inc(S["const_in"], 16)
            sp.dma_start(cos_t[:, :], io["cos"]).then_inc(S["const_in"], 16)
            sp.dma_start(sin_t[:, :], io["sin"]).then_inc(S["const_in"], 16)
            sp.dma_start(iota16[:, :], io["iota16"].partition_broadcast(P)).then_inc(S["const_in"], 16)
            sp.dma_start(x[:, :, :], io["x"].rearrange("(c p) d -> p c d", p=P)).then_inc(S["x_in"], 16)

            def load_half(n, half):
                sp.dma_start(ada_w[:, half], io["ada_w"][bass.ds(2 * n + half, 1)]
                             .rearrange("a p k n -> p (a k) n")).then_inc(ada_in[half], 16)

            sp.wait_ge(S["zeros_done"], 1)
            sp.dma_start(bias_first[0:1, :, :], io["ada_b"][0:1, 0:FIRST_BLOCKS * 512]
                         .rearrange("a (b n) -> a b n", b=FIRST_BLOCKS)).then_inc(S["bias_in"], 16)
            for n in range(FIRST_BLOCKS):
                for half in range(2):
                    if n:
                        sp.wait_ge(S["acc_done"], 2 * n + half - 1)
                    load_half(n, half)

            def load_g(l, which):
                sp.wait_ge(S["norm_gain"], l * 2 + which + 1)
                park()
                sp.dma_start(g_row[:, :], io["norm_g"][bass.ds(l * 2 + which, 1), :]
                             .partition_broadcast(P).rearrange("p a d -> p (a d)")).then_inc(S["g_in"], 16)

            with sp.Fori(0, DEPTH) as l:
                sp.wait_ge(S["layer_done"], l + 1)
                park()
                sp.dma_start(lam_raw[:, :, :], io["lam"][bass.ds(l, 1)].partition_broadcast(P)
                             .rearrange("p a b c -> p (a b) c")).then_inc(S["small_in"], 16)
                sp.dma_start(g_sub[:, :], io["g_sub"][bass.ds(l, 1), :].partition_broadcast(P)
                             .rearrange("p a d -> p (a d)")).then_inc(S["small_in"], 16)
                sp.dma_start(gate_b[:, :], io["gate_b"][bass.ds(l, 1)]
                             .rearrange("a p m -> p (a m)")).then_inc(S["small_in"], 16)
                load_g(l, 0)
                sp.wait_ge(S["zeros_done"], l + 2)
                park()
                with sp.Fori(0, TURNS) as t:
                    i = l * TURNS + t
                    n0 = FIRST_BLOCKS + TURN_BLOCKS * i

                    def load_w(g):
                        sp.wait_ge(proj[g], i + 1)
                        park()
                        sp.dma_start(w_qkv[:, g], io["w_qkv"][bass.ds(i * 6 + g, 1)]
                                     .rearrange("a p k n -> p (a k) n")).then_inc(w_in[g], 16)

                    load_w(0)
                    for half in range(2):
                        sp.wait_ge(S["acc_done"], 2 * n0 + half - 1)
                        park()
                        load_half(n0, half)
                        load_w(half + 1)
                    sp.dma_start(bias0[0:1, :, :], io["ada_b"][:, bass.ds(n0 * 512, TURN_BLOCKS * 512)]
                                 .rearrange("a (b n) -> a b n", b=TURN_BLOCKS)).then_inc(S["bias_in"], 16)
                    for g in range(3, 6):
                        load_w(g)
                    for b in range(1, TURN_BLOCKS):
                        for half in range(2):
                            sp.wait_ge(S["acc_done"], 2 * n0 + 2 * b + half - 1)
                            park()
                            load_half(n0 + b, half)
                load_g(l, 1)
                sp.wait_ge(proj[5], TURNS * l + TURNS + 1)
                park()
                with sp.Fori(0, MT // 2) as m2:
                    for s in range(2):
                        sp.wait_ge(m_mm[s], 4 * (l * (MT // 2) + m2) + 4)
                        park()
                        sp.dma_start(w_m[:, s], io["w_m"][bass.ds(l * MT + m2 * 2 + s, 1)]
                                     .rearrange("a p k n -> p (a k) n")).then_inc(m_in[s], 16)
                    sp.wait_ge(S["yd_ev"], TURNS * l + TURNS + 1)
                    park()
                    sp.dma_start(w_out[:, bass.ds(m2 * 2, 2), :], io["w_out"][bass.ds(l, 1), :, bass.ds(m2 * 2, 2)]
                                 .rearrange("a p k n -> p (a k) n")).then_inc(S["wout_in"], 16)
                sp.wait_ge(S["wo_done"], 2 * CH * l + 2 * CH)
                park()
                with sp.Fori(0, HEADS) as hq:
                    for c in range(2):
                        n = (l * HEADS + hq) * 2 + c
                        sp.wait_ge(S["sc_done"], n + 1)
                        park()
                        sp.dma_start(q_w[:, c], io["w_q"][bass.ds(n, 1)]
                                     .rearrange("a p k n -> p (a k) n")).then_inc(q_in[c], 16)
            sp.wait_ge(S["layer_done"], DEPTH + 1)
            park()
            sp.dma_start(g_row[:, :], io["final_g"].partition_broadcast(P)).then_inc(S["g_in"], 16)
            for ch in range(CH):
                sp.wait_ge(S["out_ready"], ch + 1)
                sp.dma_start(out.rearrange("b (c p) d -> p (b c) d", p=P)[:, ch, :], h2[:, ch, :]).then_inc(S["out_done"], 16)
            sp.wait_ge(S["out_done"], 16 * CH)

        @block.tensor
        def _(pe):
            def park():
                pe.sem_inc(S["parked_pe"], 1)

            for g in range(6):
                pe.sem_inc(proj[g], 1)
            for s in range(2):
                pe.sem_inc(m_mm[s], 4)
            pe.sem_inc(S["pv_done"], 2)
            pe.sem_inc(S["y_done"], 2)
            pe.sem_inc(S["sc_done"], 2)
            pe.sem_inc(S["v_pe"], 1)
            pe.wait_ge(S["const_in"], 5 * 16)
            pe.wait_ge(S["c_act_done"], 1)

            def mod_block(n, slot):
                pe.wait_ge(S["acc_done"], 2 * n + 2)
                pe.wait_ge(S["mod_evac"], n)
                pe.matmul(ps[:, 6, :], ones[:, :], mod_acc[:, slot, :], start=True, stop=True).then_inc(S["mod_mm"], 1)

            def norm(l, which, h):
                for ch in range(CH):
                    n = l * 2 * CH + which * CH + ch
                    pe.wait_ge(S["norm_h"], n + 1)
                    for half in range(2):
                        bank = 2 * (ch % 2) + half
                        if ch >= 2:
                            pe.wait_ge(S["hT_ev"], 2 * n + half - 3)
                        for k in range(4):
                            kk = 4 * half + k
                            last = pe.transpose(ps[:, bank, k * P:(k + 1) * P], h[:, ch, kk * P:(kk + 1) * P], C(IDENT))
                        last.then_inc(S["tr_done"], 1)

            def project(i, g, bank):
                pe.wait_ge(w_in[g], 16 * i + 16)
                for k in range(KD):
                    last = pe.matmul(ps[:, bank, :], w_qkv[:, g, k, :], hT[:, k, :], start=(k == 0), stop=(k == KD - 1))
                last.then_inc(proj[g], 1)

            def query(l, head, c):
                n = (l * HEADS + head) * 2 + c
                pe.wait_ge(q_in[c], 16 * (l * HEADS + head) + 16)
                pe.wait_ge(S["qst_ev"], n + 1)
                for k in range(KD):
                    last = pe.matmul(ps[:, 2 + c, :], q_w[:, c, k, :], hT[:, k, :], start=(k == 0), stop=(k == KD - 1))
                last.then_inc(S["query_done"], 1)

            def head_scores(l, head):
                for c in range(2):
                    n = (l * HEADS + head) * 2 + c
                    pe.wait_ge(S["qst_ev"], n + 3)
                    pe.wait_ge(S["sc_ev"], n + 1)
                    for ch in range(CH):
                        last = pe.matmul(ps[:, 4 + c, ch * P:(ch + 1) * P], q_st[:, c, ch * P:(ch + 1) * P],
                                         q_w[:, c, KD, :], start=True, stop=True)
                    last.then_inc(S["sc_done"], 1)

            def peer_head(l, hd, last_head):
                for ch in range(CH):
                    if not last_head and ch < 2:
                        query(l, hd + 1, ch)
                    if not last_head and ch == 2:
                        head_scores(l, hd + 1)
                    J = (l * HEADS + hd) * CH + ch
                    pe.wait_ge(S["v_added"], J + 1)
                    pe.wait_ge(S["diag_done"], 8 * J + 8)
                    for k in range(V_PE):
                        pe.wait_ge(v_in[k], 32 * J + 16)
                        for n in range(2):
                            last = pe.matmul(ps[:, n, :], diag[:, k, :], ring_v[:, k, n * 512:(n + 1) * 512],
                                             start=(k == 0), stop=(k == V_PE - 1))
                        last.then_inc(S["v_pe"], 1)

            def project_v(g, bank, chunks):
                for c in chunks:
                    for k in range(KD):
                        last = pe.matmul(ps[:, bank, c * P:(c + 1) * P], hT[:, k, c * P:(c + 1) * P],
                                         w_qkv[:, g, k, :], start=(k == 0), stop=(k == KD - 1))
                return last

            def mix(i):
                pe.wait_ge(S["dq_ready"], i + 1)
                project(i, 0, 0)
                n0 = FIRST_BLOCKS + TURN_BLOCKS * i
                mod_block(n0, 0)
                pe.wait_ge(S["dk_ready"], i + 1)
                project(i, 1, 1)
                mod_block(n0 + 1, 1)
                pe.wait_ge(w_in[2], 16 * i + 16)
                pe.wait_ge(S["yd_ev"], i + 1)
                project_v(2, 7, range(CH)).then_inc(proj[2], 1)
                mod_block(n0 + 2, 2)

                def piece(u):
                    if u == 0:
                        pe.wait_ge(S["q_ev"], i + 1)
                        project(i, 3, 0)
                    if u == 2:
                        pe.wait_ge(S["k_ev"], i + 1)
                        project(i, 4, 1)
                    if u == 4:
                        pe.wait_ge(w_in[5], 16 * i + 16)
                        pe.wait_ge(S["v_ev"], i + 1)
                    if 4 <= u < 8:
                        last = project_v(5, 7, [u - 4])
                        if u == 7:
                            last.then_inc(proj[5], 1)
                    if u == 5:
                        pe.wait_ge(S["dqraw_ev"], i + 1)
                        pe.matmul(ps[:, 0, :], C(ROPE_PERM), dq_raw, start=True, stop=True).then_inc(S["rope_mm"], 1)
                    if u == 6:
                        pe.wait_ge(S["dkraw_ev"], i + 1)
                        pe.matmul(ps[:, 1, :], C(ROPE_PERM), dk_raw, start=True, stop=True).then_inc(S["rope_mm"], 1)

                def logits(u, bank, stop):
                    h, kb = u // CH, CH - 1 - u % CH
                    r = slice(HD * h, HD * h + HD)
                    return pe.matmul(ps[:, bank, 0:qcols(kb)], sb_k[r, kb * P:(kb + 1) * P], sb_q[r, kb * P:SEQ],
                                     start=True, stop=stop)

                for u in range(2 * CH + 2):
                    if u < 2 * CH:
                        if u == 0:
                            pe.wait_ge(S["q_ev"], i + 1)
                            pe.wait_ge(S["k_ev"], i + 1)
                        if u < 2:
                            pe.wait_ge(S["p_exp"], 8 * i + 1)
                        else:
                            pe.wait_ge(S["L_done"], 8 * i + u - 1)
                        logits(u, 2 + u % 2, True).then_inc(S["z_done"], 1)
                        piece(u)
                    if 1 <= u <= 2 * CH:
                        b = u - 1
                        h, kb = b // CH, CH - 1 - b % CH
                        pe.wait_ge(S["L_done"], 8 * i + b + 1)
                        if b < 2:
                            pe.wait_ge(S["wt_ev"], CH * i + 1)
                        else:
                            pe.wait_ge(S["w_exp"], 8 * i + b - 1)
                        bank = 4 + b % 2
                        logits(b, bank, False)
                        last = pe.matmul(ps[:, bank, 0:qcols(kb)], C(NEG_UPPER), L[:, h, kb, 0:qcols(kb)],
                                         start=False, stop=(kb == CH - 1))
                        for kk in range(kb + 1, CH):
                            last = pe.matmul(ps[:, bank, (kk - kb) * P:qcols(kb)], C(NEG_ONES),
                                             L[:, h, kk, 0:qcols(kk)], start=False, stop=(kk == CH - 1))
                        last.then_inc(S["b_done"], 1)
                    if u >= 2:
                        b = u - 2
                        h, kb = b // CH, CH - 1 - b % CH
                        pe.wait_ge(S["w_masked"], 8 * i + b + 1)
                        if b == 0:
                            pe.wait_ge(S["v_ev"], i + 1)
                            pe.wait_ge(S["mod_evac"], n0 + TURN_BLOCKS)
                        pe.matmul(ps[HD * h:HD * h + HD, 6, kb * P:SEQ], sb_v[:, kb * P + HD * h:kb * P + HD * h + HD],
                                  w_att[:, b % 2, 0:qcols(kb)], start=(kb == CH - 1), stop=(kb == 0),
                                  skip_group_check=True).then_inc(S["pv_done"], 1)

                pe.wait_ge(S["dq_ready"], i + 2)
                pe.wait_ge(S["dk_ready"], i + 2)
                for step in range(CH + 3):
                    if step < CH:
                        for c in range(2):
                            v = 2 * step + c
                            if v >= 2:
                                pe.wait_ge(S["p_exp"], 8 * i + v)
                            r = slice(HD * c, HD * c + HD)
                            pe.matmul(ps[:, 2 + c, 0:(step + 1) * P], dq[r, step * P:(step + 1) * P],
                                      dk[r, 0:(step + 1) * P], start=True, stop=True).then_inc(S["s_done"], 1)
                    if 1 <= step <= CH:
                        q = step - 1
                        pe.wait_ge(S["dw_done"], CH * i + q + 1)
                        if q < 2:
                            pe.wait_ge(S["w_exp"], 8 * i + 8)
                        else:
                            pe.wait_ge(S["wt_ev"], CH * i + q)
                        for kb in range(q + 1):
                            last = pe.transpose(ps[:, 4 + q % 2, kb * P:(kb + 1) * P],
                                                prob[:, 2 * (q % 2), kb * P:(kb + 1) * P], C(IDENT))
                        last.then_inc(S["wt_done"], 1)
                    if 2 <= step <= CH + 1:
                        q = step - 2
                        pe.wait_ge(S["wt_ev"], CH * i + q + 2)
                        if q == 0:
                            pe.wait_ge(S["ysb_ev"], i + 1)
                            pe.wait_ge(S["dv_ev"], i + 1)
                        for kb in range(q + 1):
                            last = pe.matmul(ps[:, Y_BANK[q], q * P:(q + 1) * P], w_t[:, q % 2, kb * P:(kb + 1) * P],
                                             d_v[:, kb * P:(kb + 1) * P], start=(kb == 0), stop=(kb == q))
                        last.then_inc(S["y_done"], 1)
                    if step >= 3:
                        q = step - 3
                        pe.wait_ge(S["yn_done"], CH * i + q + 1)
                        pe.transpose(ps[:, 7, q * P:(q + 1) * P], y_n[:, q % 2, :], C(IDENT)).then_inc(S["yt_done"], 1)

            for n in range(FIRST_BLOCKS):
                mod_block(n, n % TURN_BLOCKS)
            with pe.Fori(0, DEPTH) as l:
                norm(l, 0, h1)
                pe.wait_ge(S["hT_ev"], 4 * CH * l + 2 * CH)
                park()
                with pe.Fori(0, TURNS) as t:
                    mix(l * TURNS + t)
                pe.wait_ge(S["yd_ev"], TURNS * l + TURNS + 1)
                park()
                with pe.Fori(0, MT // 2) as m2:
                    for s in range(2):
                        m = l * MT + m2 * 2 + s
                        pe.wait_ge(m_in[s], 16 * (l * (MT // 2) + m2) + 16)
                        pe.wait_ge(S["merged_done"], m + 1)
                        for b, (k0, n, rhs) in enumerate(((0, KD, hT), (KD, KD, hT), (16, 4, y_sb), (20, 4, y_d))):
                            for k in range(n):
                                last = pe.matmul(ps[:, 4 * s + b, :], w_m[:, s, k0 + k, :], rhs[:, k, :],
                                                 start=(k == 0), stop=(k == n - 1))
                            last.then_inc(m_mm[s], 1)
                pe.wait_ge(S["merged_done"], MT * l + MT + 2)
                pe.wait_ge(S["wout_in"], 64 * l + 64)
                for c in range(CH):
                    for n in range(2):
                        for k in range(KD):
                            last = pe.matmul(ps[:, 2 * c + n, :], merged[:, k, c * P:(c + 1) * P],
                                             w_out[:, k, n * 512:(n + 1) * 512], start=(k == 0), stop=(k == KD - 1))
                        last.then_inc(S["wo_done"], 1)
                norm(l, 1, h2)
                pe.wait_ge(S["hT_ev"], 4 * CH * l + 4 * CH)
                park()
                query(l, 0, 0)
                query(l, 0, 1)
                head_scores(l, 0)
                with pe.Fori(0, HEADS - 1) as hd:
                    peer_head(l, hd, False)
                peer_head(l, HEADS - 1, True)

        @block.scalar
        def _(act):
            def park():
                act.sem_inc(S["parked_act"], 1)

            def start_root(dst, total, n):
                act.drain()
                act.activation(dst, total, ACT.Ln, scale=1.0 / n, bias=eps[:, :])
                act.drain()
                return act.activation(dst, dst, ACT.Exp, scale=-0.5)

            act.sem_inc(S["p_exp"], 1)
            act.sem_inc(S["wt_ev"], 1)
            act.sem_inc(S["yd_ev"], 1)
            act.sem_inc(S["qst_ev"], 2)
            act.sem_inc(S["sc_ev"], 2)
            act.wait_ge(S["const_in"], 5 * 16)
            act.activation(c_sig[:, :], c_raw[:, :], ACT.Sigmoid).then_inc(S["c_sig_done"], 1)

            def mod_evac(n, place):
                act.wait_ge(S["mod_mm"], n + 1)
                park()
                act.copy(mod[:, :, :].rearrange("p a d -> p (a d)")[:, bass.ds(place * 512, 512)],
                         ps[:, 6, :]).then_inc(S["mod_evac"], 1)

            def norm(l, which):
                for ch in range(CH):
                    if which:
                        act.wait_ge(S["x_upd"], 2 * CH * l + 2 * ch + 2)
                    act.activation(h_row[:, :], x[:, ch, :], ACT.Square, accum_out=ss[:, ch:ch + 1])
                    act.drain()
                start_root(root0[:, :], ss[:, :], D).then_inc(S["sq_done"], 1)
                for ch in range(CH):
                    for half in range(2):
                        act.wait_ge(S["tr_done"], 2 * (l * 2 * CH + which * CH + ch) + half + 1)
                        act.copy(hT[:, 4 * half:4 * half + 4, ch * P:(ch + 1) * P],
                                 ps[:, 2 * (ch % 2) + half, :].rearrange("p (k n) -> p k n", k=4)).then_inc(S["hT_ev"], 1)

            def stage_query(l, head, c):
                n = (l * HEADS + head) * 2 + c
                act.wait_ge(S["query_done"], n + 1)
                act.wait_ge(S["sc_done"], n + 1)
                act.copy(q_st[:, c, :], ps[:, 2 + c, :]).then_inc(S["qst_ev"], 1)

            def stage_scores(l, head):
                for c in range(2):
                    act.wait_ge(S["sc_done"], (l * HEADS + head) * 2 + c + 3)
                    act.copy(scores[:, :, c, :], ps[:, 4 + c, :].rearrange("p (c n) -> p c n", c=CH)
                             ).then_inc(S["sc_ev"], 1)

            def peer_head(l, hd, last_head):
                for ch in range(CH):
                    J = (l * HEADS + hd) * CH + ch
                    act.wait_ge(S["topk_done"], J + 1)
                    act.activation(gexp, best, ACT.Exp, bias=nbest, accum_out=gsum).then_inc(S["gate_exp"], 1)
                    if not last_head and ch < 2:
                        stage_query(l, hd + 1, ch)
                    if not last_head and ch == CH - 1:
                        stage_scores(l, hd + 1)
                    act.wait_ge(S["dots_done"], J + 1)
                    act.activation(gel, dots, ACT.Gelu).then_inc(S["gelu_done"], 1)
                    act.wait_ge(S["coef_done"], J + 1)
                    act.wait_ge(S["v_pe"], 8 * J + 1)
                    for k in range(V_PE):
                        act.activation(diag[:, k, :], C(IDENT), ACT.Copy, scale=coef[:, k:k + 1]).then_inc(S["diag_done"], 1)

            def mix(i, t):
                act.wait_ge(proj[0], i + 2)
                act.mul(sb_q, ps[:, 0, :], SCALE).then_inc(S["q_ev"], 1)
                n0 = FIRST_BLOCKS + TURN_BLOCKS * i
                mod_evac(n0, TURN_BLOCKS * t)
                mod_evac(n0 + 1, TURN_BLOCKS * t + 1)
                act.wait_ge(proj[2], i + 2)
                act.copy(sb_v, ps[:, 7, :]).then_inc(S["v_ev"], 1)
                mod_evac(n0 + 2, TURN_BLOCKS * t + 2)
                for u in range(2 * CH + 1):
                    if u < 2 * CH:
                        n = qcols(CH - 1 - u % CH)
                        act.wait_ge(S["z_done"], 8 * i + u + 1)
                        if u >= 2:
                            act.wait_ge(S["L_done"], 8 * i + u - 1)
                        act.activation(soft[:, u % 2, 0:n], ps[:, 2 + u % 2, 0:n], ACT.Abs)
                        act.drain()
                        act.activation(soft[:, u % 2, 0:n], soft[:, u % 2, 0:n], ACT.Exp, scale=-1.0)
                        act.drain()
                        act.activation(soft[:, u % 2, 0:n], soft[:, u % 2, 0:n], ACT.Ln, bias=1.0).then_inc(S["ln_done"], 1)
                    if u == 2:
                        act.wait_ge(proj[3], i + 2)
                        act.mul(dq_raw, ps[:, 0, :], SCALE).then_inc(S["dqraw_ev"], 1)
                    if u == 4:
                        act.wait_ge(proj[4], i + 2)
                        act.copy(dk_raw, ps[:, 1, :]).then_inc(S["dkraw_ev"], 1)
                    if u >= 1:
                        b = u - 1
                        n = qcols(CH - 1 - b % CH)
                        act.wait_ge(S["b_done"], 8 * i + b + 1)
                        act.wait_ge(S["pv_done"], 8 * i + b + 1)
                        act.activation(w_att[:, b % 2, 0:n], ps[:, 4 + b % 2, 0:n], ACT.Exp).then_inc(S["w_exp"], 1)
                act.wait_ge(proj[5], i + 2)
                act.copy(d_v, ps[:, 7, :]).then_inc(S["dv_ev"], 1)
                for step in range(CH + 2):
                    if step < CH:
                        for c in range(2):
                            v = 2 * step + c
                            n = (step + 1) * P
                            act.wait_ge(S["max_done"], 8 * i + v + 1)
                            if step >= 2:
                                act.wait_ge(S["wt_done"], CH * i + step - 1)
                            act.activation(prob[:, 2 * (step % 2) + c, 0:n], ps[:, 2 + c, 0:n], ACT.Exp,
                                           bias=nmax[:, v:v + 1], accum_out=zsum[:, v:v + 1]).then_inc(S["p_exp"], 1)
                    if 1 <= step <= CH:
                        q = step - 1
                        act.wait_ge(S["wt_done"], CH * i + q + 1)
                        act.wait_ge(S["y_done"], CH * i + q + 1)
                        act.copy(w_t[:, q % 2, 0:(q + 1) * P], ps[:, 4 + q % 2, 0:(q + 1) * P]).then_inc(S["wt_ev"], 1)
                    if step >= 2:
                        q = step - 2
                        act.wait_ge(S["y_done"], CH * i + q + 3)
                        act.activation(junk_y, ps[:, Y_BANK[q], q * P:(q + 1) * P], ACT.Square,
                                       accum_out=yss[:, q:q + 1])
                        start_root(yroot0[:, q:q + 1], yss[:, q:q + 1], P).then_inc(S["y_sq"], 1)
                act.wait_ge(S["yt_done"], CH * i + CH)
                park()
                act.copy(y_d[:, bass.ds(t, 1), :].rearrange("p a n -> p (a n)"), ps[:, 7, :]).then_inc(S["yd_ev"], 1)

            act.preload_act_table_set("natural_log_exp_and_others")
            for n in range(FIRST_BLOCKS):
                mod_evac(n, MOD_BLOCKS - FIRST_BLOCKS + n)
            act.wait_ge(S["x_in"], 16)
            with act.Fori(0, DEPTH) as l:
                act.wait_ge(S["layer_done"], l + 1)
                park()
                act.preload_act_table_set("natural_log_exp_and_others")
                norm(l, 0)
                act.wait_ge(S["lam_summed"], l + 1)
                act.activation(lam_exp[:, :], lam_sum[:, :], ACT.Exp).then_inc(S["lam_exped"], 1)
                with act.Fori(0, TURNS) as t:
                    mix(l * TURNS + t, t)
                with act.Fori(0, MT // 2) as m2:
                    for s in range(2):
                        m = l * MT + m2 * 2 + s
                        act.wait_ge(S["merged_done"], m + 1)
                        for b in range(2):
                            act.wait_ge(m_mm[s], 4 * (l * (MT // 2) + m2) + b + 5)
                            park()
                            act.activation(sig[:, s, b, :], ps[:, 4 * s + b, :], ACT.Sigmoid,
                                           bias=gate_b[:, bass.ds(b * MT + m2 * 2 + s, 1)]).then_inc(S["sig_done"], 1)
                act.preload_act_table_set("natural_log_exp_and_others")
                norm(l, 1)
                stage_query(l, 0, 0)
                stage_query(l, 0, 1)
                stage_scores(l, 0)
                with act.Fori(0, HEADS - 1) as hd:
                    peer_head(l, hd, False)
                peer_head(l, HEADS - 1, True)
            act.preload_act_table_set("natural_log_exp_and_others")
            act.wait_ge(S["layer_done"], DEPTH + 1)
            for ch in range(CH):
                act.activation(h_row[:, :], x[:, ch, :], ACT.Square, accum_out=ss[:, ch:ch + 1])
                act.drain()
            start_root(root0[:, :], ss[:, :], D).then_inc(S["out_sq"], 1)

        @block.gpsimd
        def _(pool):
            def park():
                pool.sem_inc(S["parked_pool"], 1)

            with pool.Fori(0, DEPTH) as l:
                with pool.Fori(0, TURNS) as t:
                    i = l * TURNS + t
                    for u in range(2 * CH):
                        pool.wait_ge(S["w_exp"], 8 * i + u + 1)
                        park()
                        pool.affine_select(out=w_att[:, u % 2, 0:P], in_=w_att[:, u % 2, 0:P], compare_op=ALU.is_gt,
                                           fill=0.0, base=0, pattern=[[1, P]], channel_multiplier=-1
                                           ).then_inc(S["w_masked"], 1)
                with pool.Fori(0, CH * HEADS) as j:
                    J = l * CH * HEADS + j
                    pool.wait_ge(S["topk_done"], J + 1)
                    pool.wait_ge(S["u_used"], 2 * RING * J + RING)
                    park()
                    pool.tensor_copy(idx_u[:, :], idx_next[:, :]).then_inc(S["idx_u_set"], 1)
                    pool.wait_ge(S["idx_u_set"], J + 1)
                    for k in range(TOPK):
                        pool.wait_ge(S["u_used"], TOPK * J + k + 1)
                        park()
                        pool.indirect_dma_start(out=ring_u[:, k % RING, :], out_offset=None, in_=io["u"],
                                                in_offset=bass.IndirectOffsetOnAxis(ap=idx_u[:, k:k + 1], axis=0)
                                                ).then_inc(u_in[k % RING], 16)
                    pool.wait_ge(S["v_dve"], RING * J + RING)
                    park()
                    pool.tensor_copy(idx_v[:, :], idx_next[:, :]).then_inc(S["idx_taken"], 1)
                    pool.wait_ge(S["idx_taken"], J + 1)
                    for k in range(TOPK):
                        if k < RING:
                            pool.wait_ge(S["v_dve"], RING * J + k + 1)
                        else:
                            pool.wait_ge(S["v_pe"], RING * J + k - RING + 2)
                        park()
                        pool.indirect_dma_start(out=ring_v[:, k % RING, :], out_offset=None, in_=io["v"],
                                                in_offset=bass.IndirectOffsetOnAxis(ap=idx_v[:, k:k + 1], axis=0)
                                                ).then_inc(v_in[k % RING], 16)

        @block.vector
        def _(dve):
            def park():
                dve.sem_inc(S["parked_dve"], 1)

            dve.memset(ones[:, :], 1.0)
            dve.memset(eps[:, :], EPS)
            for i in range(DEPTH):
                dve.memset(lam_init[:, i:i + 1], LAM_INIT[i])
                dve.memset(lam_rest[:, i:i + 1], 1.0 - LAM_INIT[i])
                dve.memset(expert0[:, i:i + 1], float(i * N_EXPERTS))
            for name, n in (("layer_done", 1), ("norm_gain", 1), ("dq_ready", 1), ("dk_ready", 1),
                            ("merged_done", 2), ("v_added", 1), ("u_used", RING), ("v_dve", RING)):
                dve.sem_inc(S[name], n)
            dve.memset(bias_first, 0.0).then_inc(S["zeros_done"], 1)
            dve.wait_ge(S["c_sig_done"], 1)
            dve.tensor_tensor(c_act[:, :], c_sig[:, :], c_raw[:, :], ALU.mult)
            dve.drain().then_inc(S["c_act_done"], 1)

            def mod_acc_block(n, slot, bias):
                for half in range(2):
                    dve.wait_ge(ada_in[half], 16 * n + 16)
                    cols = slice(half * 256, half * 256 + 256)
                    acc = mod_acc[:, slot, cols]
                    for k in range(KD):
                        last = dve.scalar_tensor_tensor(acc, ada_w[:, half, k, :], c_act[:, k:k + 1],
                                                        bias[:, cols] if k == 0 else acc, ALU.mult, ALU.add)
                        if k < KD - 1:
                            dve.drain()
                    last.then_inc(S["acc_done"], 1)

            def inv_root_mean(dst, start, total, n):
                width = dst.shape[-1]
                a, b = newton[:, 0, 0:width], newton[:, 1, 0:width]
                dve.tensor_scalar(a, total, 1.0 / n, EPS, ALU.mult, ALU.add)
                dve.tensor_tensor(b, start, start, ALU.mult)
                dve.drain()
                dve.tensor_tensor(a, a, b, ALU.mult)
                dve.drain()
                dve.tensor_scalar(a, a, -0.5, 1.5, ALU.mult, ALU.add)
                dve.drain()
                dve.tensor_tensor(dst, start, a, ALU.mult)
                dve.drain()

            def norm(l, which, h):
                shift, gain = (mod[:, SHIFT2, :], mod[:, GAIN2, :]) if which else (mod[:, SHIFT1, :], mod[:, GAIN1, :])
                dve.wait_ge(S["g_in"], 32 * l + 16 * which + 16)
                dve.wait_ge(S["mod_evac"], l * MOD_BLOCKS + (MOD_BLOCKS if which else 0) + FIRST_BLOCKS)
                dve.scalar_tensor_tensor(gain, gain, 1.0, g_row[:, :], ALU.add, ALU.mult).then_inc(S["norm_gain"], 1)
                dve.wait_ge(S["sq_done"], 2 * l + which + 1)
                inv_root_mean(rstd[:, :], root0[:, :], ss[:, :], D)
                for ch in range(CH):
                    dve.scalar_tensor_tensor(h[:, ch, :], x[:, ch, :], rstd[:, ch:ch + 1], gain, ALU.mult, ALU.mult)
                    dve.drain()
                    dve.tensor_tensor(h[:, ch, :], h[:, ch, :], shift, ALU.add).then_inc(S["norm_h"], 1)

            def rope(i, which, raw, dst, bank, done):
                if which:
                    dve.wait_ge(S["dkraw_ev"], i + 1)
                else:
                    dve.wait_ge(S["dqraw_ev"], i + 1)
                dve.tensor_tensor(rope_tmp[:, 0, :], raw, cos_t[:, :], ALU.mult)
                dve.wait_ge(S["rope_mm"], 2 * i + which + 1)
                dve.tensor_tensor(rope_tmp[:, 1, :], ps[:, bank, :], sin_t[:, :], ALU.mult)
                dve.drain()
                dve.tensor_tensor(dst, rope_tmp[:, 0, :], rope_tmp[:, 1, :], ALU.add).then_inc(S[done], 1)
                dve.drain()

            def mix(i, t):
                n0 = FIRST_BLOCKS + TURN_BLOCKS * i
                dve.wait_ge(S["bias_in"], 16 * i + 32)
                for b in range(TURN_BLOCKS):
                    mod_acc_block(n0 + b, b, bias0[:, b, :])
                    if b == 1:
                        dve.wait_ge(proj[1], i + 2)
                        dve.tensor_copy(sb_k, ps[:, 1, :]).then_inc(S["k_ev"], 1)
                for u in range(2 * CH + 1):
                    if u >= 1:
                        b = u - 1
                        h, kb = b // CH, CH - 1 - b % CH
                        n = qcols(kb)
                        dve.wait_ge(S["ln_done"], 8 * i + b + 1)
                        dve.scalar_tensor_tensor(L[:, h, kb, 0:n], ps[:, 2 + b % 2, 0:n], 0.0, soft[:, b % 2, 0:n],
                                                 ALU.max, ALU.add)
                        dve.drain()
                        dve.tensor_tensor(L[:, h, kb, 0:P], L[:, h, kb, 0:P], C(STRICT), ALU.mult).then_inc(S["L_done"], 1)
                        dve.drain()
                    if u == 6:
                        rope(i, 0, dq_raw, dq, 0, "dq_ready")
                    if u == 7:
                        rope(i, 1, dk_raw, dk, 1, "dk_ready")
                dve.wait_ge(S["pv_done"], 8 * i + 8 + 2)
                dve.tensor_copy(y_sb[:, bass.ds(t, 1), :].rearrange("p a n -> p (a n)"), ps[:, 6, :]).then_inc(S["ysb_ev"], 1)
                for step in range(CH + 3):
                    if step < CH:
                        for c in range(2):
                            v = 2 * step + c
                            dve.wait_ge(S["s_done"], 8 * i + v + 1)
                            dve.tensor_tensor(ps[:, 2 + c, step * P:(step + 1) * P], ps[:, 2 + c, step * P:(step + 1) * P],
                                              C(NEG_MASK), ALU.add)
                            dve.drain()
                            dve.tensor_reduce(nmax[:, v:v + 1], ps[:, 2 + c, 0:(step + 1) * P], AX.X, ALU.max,
                                              negate=True).then_inc(S["max_done"], 1)
                    if 1 <= step <= CH:
                        q = step - 1
                        n = (q + 1) * P
                        p0, p1 = prob[:, 2 * (q % 2), 0:n], prob[:, 2 * (q % 2) + 1, 0:n]
                        dve.wait_ge(S["p_exp"], 8 * i + 2 * q + 3)
                        dve.reciprocal(rz[:, 2 * q:2 * q + 2], zsum[:, 2 * q:2 * q + 2])
                        dve.drain()
                        dve.tensor_scalar(p1, p1, rz[:, 2 * q + 1:2 * q + 2], neg_lam[:, 0:1], ALU.mult, ALU.mult)
                        dve.drain()
                        dve.scalar_tensor_tensor(p0, p0, rz[:, 2 * q:2 * q + 1], p1, ALU.mult, ALU.add).then_inc(S["dw_done"], 1)
                        dve.drain()
                    if step >= 3:
                        q = step - 3
                        dve.wait_ge(S["y_sq"], CH * i + q + 1)
                        inv_root_mean(yr[:, q:q + 1], yroot0[:, q:q + 1], yss[:, q:q + 1], P)
                        if q >= 2:
                            dve.wait_ge(S["yt_done"], CH * i + q - 1)
                        dve.scalar_tensor_tensor(y_n[:, q % 2, :], ps[:, Y_BANK[q], q * P:(q + 1) * P], yr[:, q:q + 1], g_sub[:, :],
                                                 ALU.mult, ALU.mult).then_inc(S["yn_done"], 1)

            def topk_pair(vals, idxs, src, work):
                dve.max(vals[:, 0:8], src)
                dve.drain()
                dve.max_index(idxs[:, 0:8], vals[:, 0:8], src)
                dve.match_replace(work, vals[:, 0:8], src, LOWEST)
                dve.drain()
                dve.max(vals[:, 8:16], work)
                dve.drain()
                dve.max_index(idxs[:, 8:16], vals[:, 8:16], work)

            def topk(l, ch, count):
                if count is not None:
                    dve.wait_ge(S["idx_taken"], count)
                    dve.wait_ge(S["gate_exp"], count)
                    park()
                for c in range(2):
                    topk_pair(s_top[:, c, :], i_top[:, c, :], scores[:, ch, c, :], sc_work[:, c, :])
                dve.drain()
                dve.tensor_copy(i_top_f, i_top[:, :, :])
                dve.tensor_tensor(cand, s_top[:, 0, :].unsqueeze(2).broadcast_to([P, TOPK, TOPK]),
                                  s_top[:, 1, :].unsqueeze(1).broadcast_to([P, TOPK, TOPK]), ALU.add)
                dve.drain()
                flat = cand.rearrange("p a b -> p (a b)")
                topk_pair(best, pos[:, :], flat, cand_work.rearrange("p a b -> p (a b)"))
                dve.drain()
                dve.tensor_scalar(nbest, best[:, 0:1], -1.0, None, ALU.mult)
                dve.tensor_scalar(pos_hl[:, 0, :], pos[:, :], 4, None, ALU.logical_shift_right)
                dve.tensor_scalar(pos_hl[:, 1, :], pos[:, :], 15, None, ALU.bitwise_and)
                dve.drain()
                dve.tensor_copy(pos_f, pos_hl[:, :, :])
                dve.drain()
                for c in range(2):
                    dve.tensor_tensor(onehot, pos_f[:, c, :].unsqueeze(2).broadcast_to([P, TOPK, TOPK]),
                                      iota16[:, :].unsqueeze(1).broadcast_to([P, TOPK, TOPK]), ALU.is_equal)
                    dve.drain()
                    dve.tensor_tensor(onehot, onehot, i_top_f[:, c, :].unsqueeze(1).broadcast_to([P, TOPK, TOPK]), ALU.mult)
                    dve.drain()
                    dve.tensor_reduce(sel_f[:, c, :], onehot, AX.X, ALU.add)
                    dve.drain()
                dve.scalar_tensor_tensor(sel_f[:, 0, :], sel_f[:, 0, :], float(N_KEYS), sel_f[:, 1, :], ALU.mult, ALU.add)
                dve.drain()
                dve.tensor_scalar(idx_next[:, :], sel_f[:, 0, :], expert0[:, bass.ds(l, 1)], None,
                                  ALU.add).then_inc(S["topk_done"], 1)

            for n in range(FIRST_BLOCKS):
                if n == 0:
                    dve.wait_ge(S["bias_in"], 16)
                if n == TURN_BLOCKS:
                    dve.wait_ge(S["mod_mm"], 1)
                mod_acc_block(n, n % TURN_BLOCKS, bias_first[:, n, :])
            dve.wait_ge(S["mod_mm"], FIRST_BLOCKS)
            def peer_head(l, hd, last_head):
                for ch in range(CH):
                    J = (l * HEADS + hd) * CH + ch
                    total = peer_sum[:, ch, :]
                    for k in range(TOPK):
                        dve.wait_ge(u_in[k % RING], 32 * J + 16 * (k // RING) + 16)
                        row = ring_u[:, k % RING, :]
                        dve.tensor_tensor_reduce(row, row, h2[:, ch, :], 1.0, 0.0, ALU.mult, ALU.add,
                                                 dots[:, k:k + 1]).then_inc(S["u_used"], 1)
                    dve.drain().then_inc(S["dots_done"], 1)
                    dve.wait_ge(S["gate_exp"], J + 1)
                    dve.reciprocal(rsum, gsum)
                    dve.drain()
                    dve.wait_ge(S["gelu_done"], J + 1)
                    dve.scalar_tensor_tensor(coef, gel, rsum, gexp, ALU.mult, ALU.mult).then_inc(S["coef_done"], 1)
                    if ch < CH - 1:
                        topk(l, ch + 1, J + 1)
                    elif not last_head:
                        dve.wait_ge(S["sc_ev"], 2 * (l * HEADS + hd + 1) + 4)
                        topk(l, 0, J + 1)
                    for k in range(V_PE, TOPK):
                        dve.wait_ge(v_in[k % RING], 32 * J + 32)
                        dve.scalar_tensor_tensor(total, ring_v[:, k % RING, :], coef[:, k:k + 1], total,
                                                 ALU.mult, ALU.add).then_inc(S["v_dve"], 1)
                        dve.drain()
                    dve.wait_ge(S["v_pe"], 8 * J + 8 + 1)
                    dve.tensor_tensor(total, total, ps[:, 0:2, :].rearrange("p a n -> p (a n)"),
                                      ALU.add).then_inc(S["v_added"], 1)
                    if last_head:
                        dve.drain()
                        dve.tensor_tensor(total, total, mod[:, GATE2, :], ALU.mult)
                        dve.drain()
                        dve.tensor_tensor(x[:, ch, :], x[:, ch, :], total, ALU.add)

            with dve.Fori(0, DEPTH) as l:
                dve.memset(bias0, 0.0).then_inc(S["zeros_done"], 1)
                dve.wait_ge(S["small_in"], 48 * l + 48)
                for c in range(2):
                    dve.tensor_tensor(lam_prod[:, c, :], lam_raw[:, 2 * c, :], lam_raw[:, 2 * c + 1, :], ALU.mult)
                dve.drain()
                dve.tensor_reduce(lam_sum[:, :], lam_prod[:, :, :], AX.X, ALU.add).then_inc(S["lam_summed"], 1)
                dve.tensor_scalar(g_sub[:, :], g_sub[:, :], lam_rest[:, bass.ds(l, 1)], None, ALU.mult)
                norm(l, 0, h1)
                dve.wait_ge(S["lam_exped"], l + 1)
                dve.tensor_tensor(neg_lam[:, :], lam_exp[:, 1:2], lam_exp[:, 0:1], ALU.subtract)
                dve.drain()
                dve.tensor_tensor(neg_lam[:, :], neg_lam[:, :], lam_init[:, bass.ds(l, 1)], ALU.subtract)
                with dve.Fori(0, TURNS) as t:
                    mix(l * TURNS + t, t)
                with dve.Fori(0, MT // 2) as m2:
                    for s in range(2):
                        m = l * MT + m2 * 2 + s
                        for b in range(2):
                            dve.wait_ge(S["sig_done"], 2 * m + b + 1)
                            dve.wait_ge(m_mm[s], 4 * (l * (MT // 2) + m2) + b + 7)
                            dve.tensor_tensor(sig[:, s, b, :], sig[:, s, b, :], ps[:, 4 * s + 2 + b, :], ALU.mult)
                        dve.drain()
                        dve.tensor_tensor(merged[:, bass.ds(m2 * 2 + s, 1), :].rearrange("p a n -> p (a n)"),
                                          sig[:, s, 0, :], sig[:, s, 1, :], ALU.add).then_inc(S["merged_done"], 1)
                dve.drain()
                for c in range(CH):
                    for n in range(2):
                        cols = slice(n * 512, (n + 1) * 512)
                        dve.wait_ge(S["wo_done"], 2 * CH * l + 2 * c + n + 1)
                        dve.tensor_tensor(out_tmp, ps[:, 2 * c + n, :], mod[:, GATE1, cols], ALU.mult)
                        dve.drain()
                        dve.tensor_tensor(x[:, c, cols], x[:, c, cols], out_tmp, ALU.add).then_inc(S["x_upd"], 1)
                        dve.drain()
                norm(l, 1, h2)
                dve.memset(peer_sum, 0.0)
                dve.wait_ge(S["sc_ev"], 2 * HEADS * l + 4)
                park()
                topk(l, 0, None)
                with dve.Fori(0, HEADS - 1) as hd:
                    peer_head(l, hd, False)
                peer_head(l, HEADS - 1, True)
                dve.drain().then_inc(S["layer_done"], 1)

            dve.wait_ge(S["g_in"], 32 * DEPTH + 16)
            dve.wait_ge(S["out_sq"], 1)
            inv_root_mean(rstd[:, :], root0[:, :], ss[:, :], D)
            for ch in range(CH):
                dve.scalar_tensor_tensor(h2[:, ch, :], x[:, ch, :], rstd[:, ch:ch + 1], g_row[:, :],
                                         ALU.mult, ALU.mult).then_inc(S["out_ready"], 1)


def shape_constants():
    i, j = np.arange(P)[:, None], np.arange(P)[None, :]
    const = np.zeros((P, N_CONST, P), np.float32)
    const[:, IDENT] = i == j
    const[:, NEG_UPPER] = -1.0 * (i >= j)
    const[:, NEG_ONES] = -1.0
    const[:, STRICT] = i < j
    const[:, NEG_MASK] = -1e30 * (j > i)
    half = ROT // 2
    in_head = j % HD
    const[:, ROPE_PERM] = (1.0 * ((in_head >= half) & (in_head < ROT) & (i == j - half))
                           - 1.0 * ((in_head < half) & (i == j + half)))
    inv_freq = (1.0 / (np.float32(ROPE_THETA) ** (np.arange(0, ROT, 2, dtype=np.float32) / np.float32(ROT))))
    angle = inv_freq.astype(np.float32)[:, None] * np.arange(SEQ, dtype=np.float32)[None, :]
    cos_t, sin_t = np.ones((P, SEQ), np.float32), np.zeros((P, SEQ), np.float32)
    for p in range(P):
        if p % HD < ROT:
            cos_t[p], sin_t[p] = np.cos(angle[p % half]), np.sin(angle[p % half])
    return {"const": const, "cos": cos_t, "sin": sin_t, "iota16": np.arange(TOPK, dtype=np.float32)}


def lay_out(a):
    L = DEPTH
    w_in = a["w_in"].reshape(L, KD, P, -1)
    groups = w_in[..., :6 * 512].reshape(L, KD, P, 6, TURNS, P)
    gates = w_in[..., 6 * 512:].reshape(L, KD, P, 2, MT, P)
    b_sb = a["w_branch_sb"].reshape(L, 4, P, MT, P)
    b_d = a["w_branch_diff"].reshape(L, 4, P, MT, P)
    w_m = np.concatenate([gates[:, :, :, 0], gates[:, :, :, 1], b_sb, b_d], axis=1)
    wq = a["peer_wq"].reshape(L, KD, P, 2 * HEADS, P).transpose(0, 3, 2, 1, 4)
    sub = a["peer_subkeys"].reshape(L, 2 * HEADS, N_KEYS, P).transpose(0, 1, 3, 2)[:, :, :, None, :]
    ada_w = a["ada_w"].reshape(L, KD, P, 2 * MOD_BLOCKS, 256).transpose(0, 3, 2, 1, 4).reshape(-1, P, KD, 256)
    return {
        "x": a["x"][0],
        "c": a["c"].reshape(KD, P).T,
        "norm_g": np.stack([a["norm1_g"], a["norm2_g"]], axis=1).reshape(2 * L, D),
        "ada_w": np.concatenate([ada_w, ada_w[:2 * FIRST_BLOCKS]]),
        "ada_b": np.concatenate([a["ada_b"].reshape(-1), a["ada_b"][0, :FIRST_BLOCKS * 512]])[None, :],
        "w_qkv": groups.transpose(0, 4, 3, 2, 1, 5).reshape(-1, P, KD, P),
        "w_m": w_m.transpose(0, 3, 2, 1, 4).reshape(-1, P, 24, P),
        "w_out": a["w_out"].reshape(L, KD, P, D).transpose(0, 2, 1, 3),
        "w_q": np.concatenate([wq, sub], axis=3).reshape(-1, P, KD + 1, P),
        "gate_b": a["gate_b"].reshape(L, 2 * MT, P).transpose(0, 2, 1),
        "lam": a["diff_lambda"],
        "g_sub": a["diff_subln_g"],
        "u": a["peer_u"].reshape(L * N_EXPERTS, D),
        "v": a["peer_v"].reshape(L * N_EXPERTS, D),
        "final_g": a["final_g"],
    }


def kernel(**inputs):
    import concourse.bacc as bacc
    from concourse.bass_utils import run_bass_kernel_spmd

    laid = lay_out({n: np.asarray(v) for n, v in inputs.items()})
    laid.update(shape_constants())
    nc = bacc.Bacc("TRN2", target_bir_lowering=False, num_devices=1)
    arrays, io = {}, {}
    for name, a in laid.items():
        a = np.ascontiguousarray(a)
        arrays[f"in_{name}_dram"] = a
        io[name] = nc.dram_tensor(f"in_{name}_dram", a.shape, mybir.dt.from_np(a.dtype), kind="ExternalInput").ap()
    out = nc.dram_tensor("out_dram", (1, SEQ, D), F32, kind="ExternalOutput").ap()
    build(nc, io, out)
    r = run_bass_kernel_spmd(nc, [arrays], core_ids=[0])
    return r.results[0]["out_dram"]
```

```python
import math
from contextlib import ExitStack

import numpy as np

import concourse.bass as bass
from concourse import mybir

F32 = mybir.dt.float32
U32 = mybir.dt.uint32
ALU = mybir.AluOpType
ACT = mybir.ActivationFunctionType
AX = mybir.AxisListType

P = 128
D = 1024
KD = D // P
SEQ = 512
CH = SEQ // P
DEPTH = 2
HD = 64
TURNS = 4
MT = D // P
N_KEYS = 128
N_EXPERTS = N_KEYS * N_KEYS
HEADS = 8
TOPK = 16
EPS = 1e-6
ROT = 16
ROPE_THETA = 500000.0
SCALE = 1.0 / math.sqrt(HD)
MOD_BLOCKS = 6 * D // 512
FIRST_BLOCKS = 4
TURN_BLOCKS = MOD_BLOCKS // TURNS
GATE1, SHIFT2, GAIN2, GATE2, SHIFT1, GAIN1 = range(6)
RING = 8
V_PE = 8
LOWEST = -3.0e38
LAM_INIT = [0.8 - 0.6 * math.exp(-0.3 * i) for i in range(DEPTH)]
IDENT, NEG_UPPER, NEG_ONES, STRICT, NEG_MASK, ROPE_PERM = range(6)
N_CONST = 6
Y_BANK = [6, 0, 6, 0]
OUT_BANK = [0, 2, 4, 0]
TR_BANK = [0, 2, 4, 2]

A_WQKV = 0
A_SOFT = 6144
A_W = 7168
A_QKV = 8192
A_L = 12288
A_P = 16384
A_WT = 18432
A_YN = 19456
A_ROPE = 19712
A_YSB = 20736
A_YD = 22784
A_MERGED = 24832
A_SIG = 28928
A_WOUT = 8192
A_MW = 0
A_ADAW = 24832
A_ACC = 28928
A_BIAS = 30464
A_RING = 0
A_QW = 20736
A_QST = 23040
A_OUT_TMP = 24064
A_PEER_SUM = 24832
A_TOPK = 16384
A_SCORES = 19712
A_H2 = 28928
A_ADAW2 = 32256
ARENA = 34304


def build(nc, io, out):
    with ExitStack() as ctx:
        def sb(name, shape, dt=F32):
            return ctx.enter_context(nc.sbuf_tensor(name, shape, dt))

        def sem(name):
            return ctx.enter_context(nc.semaphore(name))

        ps = ctx.enter_context(nc.psum_tensor("ps", [P, 8, 512], F32))
        x = sb("x_res", [P, CH, D])
        hT = sb("hT", [P, KD, SEQ])
        mod = sb("mod", [P, 6, D])
        g_row = sb("g_row", [P, D])
        h_row = sb("h_row", [P, D])
        const = sb("const", [P, N_CONST, P])
        ones = sb("ones", [P, P])
        cos_t = sb("cos_t", [P, SEQ])
        sin_t = sb("sin_t", [P, SEQ])
        c_raw = sb("c_raw", [P, KD])
        c_sig = sb("c_sig", [P, KD])
        c_act = sb("c_act", [P, KD])
        lam_sum = sb("lam_sum", [P, 2])
        lam_exp = sb("lam_exp", [P, 2])
        lam_init = sb("lam_init", [P, DEPTH])
        lam_rest = sb("lam_rest", [P, DEPTH])
        neg_lam = sb("neg_lam", [P, 1])
        g_sub = sb("g_sub", [P, P])
        gate_b = sb("gate_b", [P, 2 * MT])
        ss = sb("ss", [P, CH])
        root0 = sb("root0", [P, CH])
        rstd = sb("rstd", [P, CH])
        newton = sb("newton", [P, 2, CH])
        eps = sb("eps", [P, 1])
        nmax = sb("nmax", [P, 8])
        zsum = sb("zsum", [P, 8])
        rz = sb("rz", [P, 8])
        yss = sb("yss", [P, CH])
        yroot0 = sb("yroot0", [P, CH])
        yr = sb("yr", [P, CH])
        arena = sb("arena", [P, ARENA])

        def part(at, *dims):
            n = int(np.prod(dims))
            v = arena[:, at:at + n]
            if len(dims) == 2:
                v = v.rearrange("p (a b) -> p a b", a=dims[0])
            if len(dims) == 3:
                v = v.rearrange("p (a b c) -> p a b c", a=dims[0], b=dims[1])
            return v

        w_qkv = part(A_WQKV, 6, KD, P)
        soft = part(A_SOFT, 2, SEQ)
        junk_y = part(A_SOFT, P)
        lam_raw = part(A_W, 4, HD)
        lam_prod = part(A_W + 4 * HD, 2, HD)
        w_att = part(A_W, 2, SEQ)
        qkv = part(A_QKV, 8, SEQ)
        sb_q, sb_k, sb_v, dq_raw, dk_raw, dq, dk, d_v = (qkv[:, n, :] for n in range(8))
        L = part(A_L, 2, CH, SEQ)
        prob = part(A_P, 4, SEQ)
        w_t = part(A_WT, 2, SEQ)
        y_n = part(A_YN, 2, P)
        rope_tmp = part(A_ROPE, 2, SEQ)
        y_sb = part(A_YSB, TURNS, SEQ)
        y_d = part(A_YD, TURNS, SEQ)
        merged = part(A_MERGED, MT, SEQ)
        sig = part(A_SIG, 2, 2, SEQ)
        w_out = part(A_WOUT, KD, D)
        w_m = part(A_MW, 2, 24, P)
        ada_w = [part(at, KD, 256) for at in (A_ADAW, A_ADAW + KD * 256, A_ADAW2)]
        mod_acc = part(A_ACC, TURN_BLOCKS, 512)
        bias0 = part(A_BIAS, TURN_BLOCKS, 512)
        bias_first = part(A_QKV, FIRST_BLOCKS, 512)
        h1 = part(A_L, CH, D)
        out_tmp = part(A_OUT_TMP, 512)
        q_w = part(A_QW, 2, KD + 1, P)
        q_st = part(A_QST, 2, SEQ)
        ring_u = part(A_RING, RING, D)
        ring_v = part(A_RING + RING * D, RING, D)
        scores = part(A_SCORES, CH, 2, N_KEYS)
        peer_sum = part(A_PEER_SUM, CH, D)
        h2 = part(A_H2, CH, D)
        at = [A_TOPK]

        def small(*dims):
            v = part(at[0], *dims)
            at[0] += int(np.prod(dims))
            assert at[0] <= A_SCORES
            return v

        sc_work = small(2, N_KEYS)
        cand = small(TOPK, TOPK)
        cand_work = small(TOPK, TOPK)
        onehot = small(TOPK, TOPK)
        s_top = small(2, TOPK)
        i_top_f = small(2, TOPK)
        best = small(TOPK)
        pos_f = small(2, TOPK)
        sel_f = small(2, TOPK)
        gexp = small(TOPK)
        gsum = small(1)
        rsum = small(1)
        nbest = small(1)
        dots = small(TOPK)
        gel = small(TOPK)
        coef = small(TOPK)
        diag = small(V_PE, P)
        i_top = sb("i_top", [P, 2, TOPK], U32)
        pos = sb("pos", [P, TOPK], U32)
        pos_hl = sb("pos_hl", [P, 2, TOPK], U32)
        idx_next = sb("idx_next", [P, TOPK], U32)
        idx_u = sb("idx_u", [P, TOPK], U32)
        idx_v = sb("idx_v", [P, TOPK], U32)
        iota16 = sb("iota16", [P, TOPK])
        expert0 = sb("expert0", [P, DEPTH])

        S = {n: sem(n) for n in (
            "c_in const_in x_in c_sig_done c_act_done zeros_done layer_done small_in lam_summed lam_exped g_in "
            "norm_gain bias_in mod_mm mod_evac acc_done sq_done sq2_done norm_h tr_done hT_ev "
            "q_ev k_ev v_ev dqraw_ev dkraw_ev dv_mm dv_ev rope_mm dq_ready dk_ready "
            "z_done  ln_done L_done b_done w_exp w_masked pv_done ysb_ev "
            "s_done max_done p_exp dw_done wt_done wt_ev y_done y_sq yn_done yt_done yd_ev "
            "sig_done merged_done wout_in wo_done x_upd "
            "query0_done qst0_ev sc0_done sc0_ev query_done qst_ev sc_done sc_ev topk_done idx_taken gate_exp dots_done gelu_done coef_done diag_done "
            "idx_u_set u_used v_dve v_pe v_added out_sq out_ready out_done "
            "parked_act parked_dve parked_pool parked_pe parked_sp").split()}
        ada_in = [sem(f"ada_in{i}") for i in range(3)]
        w_in = [sem(f"w_in{i}") for i in range(6)]
        proj = [sem(f"proj{i}") for i in range(6)]
        m_in = [sem(f"m_in{i}") for i in range(2)]
        m_mm = [sem(f"m_mm{i}") for i in range(2)]
        q_in = [sem(f"q_in{i}") for i in range(2)]
        u_in = [sem(f"u_in{i}") for i in range(RING)]
        v_in = [sem(f"v_in{i}") for i in range(RING)]

        def C(n):
            return const[:, n, :]

        def qcols(kb):
            return SEQ - P * kb

        block = ctx.enter_context(nc.Block())

        @block.sync
        def _(sp):
            def park():
                sp.sem_inc(S["parked_sp"], 1)

            sp.dma_start(c_raw[:, :], io["c"]).then_inc(S["c_in"], 16)

            def load_constants():
                sp.dma_start(const[:, :, :], io["const"]).then_inc(S["const_in"], 16)
                sp.dma_start(cos_t[:, :], io["cos"]).then_inc(S["const_in"], 16)
                sp.dma_start(sin_t[:, :], io["sin"]).then_inc(S["const_in"], 16)
                sp.dma_start(iota16[:, :], io["iota16"].partition_broadcast(P)).then_inc(S["const_in"], 16)
                sp.dma_start(x[:, :, :], io["x"].rearrange("(c p) d -> p c d", p=P)).then_inc(S["x_in"], 16)

            def load_half(half, slot):
                sp.dma_start(ada_w[slot], io["ada_w"][bass.ds(half, 1)]
                             .rearrange("a p k n -> p (a k) n")).then_inc(ada_in[slot], 16)

            sp.wait_ge(S["zeros_done"], 1)
            sp.dma_start(bias_first[0:1, :, :], io["ada_b"][0:1, 0:FIRST_BLOCKS * 512]
                         .rearrange("a (b n) -> a b n", b=FIRST_BLOCKS)).then_inc(S["bias_in"], 16)
            for half in range(2 * FIRST_BLOCKS):
                if half >= 3:
                    sp.wait_ge(S["acc_done"], half - 2)
                load_half(half, half % 3)
                if half == 2:
                    load_constants()

            def load_g(l, which):
                sp.wait_ge(S["norm_gain"], l * 2 + which + 1)
                park()
                sp.dma_start(g_row[:, :], io["norm_g"][bass.ds(l * 2 + which, 1), :]
                             .partition_broadcast(P).rearrange("p a d -> p (a d)")).then_inc(S["g_in"], 16)

            with sp.Fori(0, DEPTH) as l:
                sp.wait_ge(S["layer_done"], l + 1)
                park()
                sp.dma_start(lam_raw[:, :, :], io["lam"][bass.ds(l, 1)].partition_broadcast(P)
                             .rearrange("p a b c -> p (a b) c")).then_inc(S["small_in"], 16)
                sp.dma_start(g_sub[:, :], io["g_sub"][bass.ds(l, 1), :].partition_broadcast(P)
                             .rearrange("p a d -> p (a d)")).then_inc(S["small_in"], 16)
                sp.dma_start(gate_b[:, :], io["gate_b"][bass.ds(l, 1)]
                             .rearrange("a p m -> p (a m)")).then_inc(S["small_in"], 16)
                load_g(l, 0)
                sp.wait_ge(S["zeros_done"], l + 2)
                park()
                with sp.Fori(0, TURNS) as t:
                    i = l * TURNS + t
                    n0 = FIRST_BLOCKS + TURN_BLOCKS * i

                    def load_turn_half(b):
                        half = 2 * n0 + b
                        sp.wait_ge(S["acc_done"], half - 2)
                        park()
                        load_half(half, (2 * FIRST_BLOCKS + b) % 3)

                    def load_w(g):
                        sp.wait_ge(proj[g], i + 1)
                        park()
                        sp.dma_start(w_qkv[:, g], io["w_qkv"][bass.ds(i * 6 + g, 1)]
                                     .rearrange("a p k n -> p (a k) n")).then_inc(w_in[g], 16)

                    for b in range(3):
                        load_w(b)
                        load_turn_half(b)
                    sp.dma_start(bias0[0:1, :, :], io["ada_b"][:, bass.ds(n0 * 512, TURN_BLOCKS * 512)]
                                 .rearrange("a (b n) -> a b n", b=TURN_BLOCKS)).then_inc(S["bias_in"], 16)
                    for g in range(3, 6):
                        load_w(g)
                    for b in range(3, 2 * TURN_BLOCKS):
                        load_turn_half(b)
                load_g(l, 1)
                sp.wait_ge(proj[5], TURNS * l + TURNS + 1)
                park()
                with sp.Fori(0, MT // 2) as m2:
                    for s in range(2):
                        sp.wait_ge(m_mm[s], 4 * (l * (MT // 2) + m2) + 4)
                        park()
                        sp.dma_start(w_m[:, s], io["w_m"][bass.ds(l * MT + m2 * 2 + s, 1)]
                                     .rearrange("a p k n -> p (a k) n")).then_inc(m_in[s], 16)
                    sp.wait_ge(S["yd_ev"], TURNS * l + TURNS + 1)
                    park()
                    sp.dma_start(w_out[:, bass.ds(m2 * 2, 2), :], io["w_out"][bass.ds(l, 1), :, bass.ds(m2 * 2, 2)]
                                 .rearrange("a p k n -> p (a k) n")).then_inc(S["wout_in"], 16)
                for s in range(2):
                    sp.wait_ge(m_mm[s], 4 * (MT // 2) * (l + 1) + 4)
                    park()
                with sp.Fori(0, HEADS) as hq:
                    for c in range(2):
                        n = (l * HEADS + hq) * 2 + c
                        sp.wait_ge(S["sc_done"], n + 1)
                        park()
                        sp.dma_start(q_w[:, c], io["w_q"][bass.ds(n, 1)]
                                     .rearrange("a p k n -> p (a k) n")).then_inc(q_in[c], 16)
            sp.wait_ge(S["layer_done"], DEPTH + 1)
            park()
            sp.dma_start(g_row[:, :], io["final_g"].partition_broadcast(P)).then_inc(S["g_in"], 16)
            for ch in range(CH):
                sp.wait_ge(S["out_ready"], ch + 1)
                sp.dma_start(out.rearrange("b (c p) d -> p (b c) d", p=P)[:, ch, :], h2[:, ch, :]).then_inc(S["out_done"], 16)
            sp.wait_ge(S["out_done"], 16 * CH)

        @block.tensor
        def _(pe):
            def park():
                pe.sem_inc(S["parked_pe"], 1)

            for g in range(6):
                pe.sem_inc(proj[g], 1)
            for s in range(2):
                pe.sem_inc(m_mm[s], 4)
            pe.sem_inc(S["pv_done"], 2)
            pe.sem_inc(S["y_done"], 2)
            pe.sem_inc(S["sc_done"], 2)
            pe.sem_inc(S["v_pe"], 1)

            def mod_block(n, slot):
                pe.wait_ge(S["acc_done"], 2 * n + 2)
                pe.wait_ge(S["mod_evac"], n)
                pe.matmul(ps[:, 6, :], ones[:, :], mod_acc[:, slot, :], start=True, stop=True).then_inc(S["mod_mm"], 1)

            def transposes(l, which, ch, h):
                n = l * 2 * CH + which * CH + ch
                pe.wait_ge(S["norm_h"], n + 1)
                for half in range(2):
                    bank = TR_BANK[ch] + half
                    if ch == 3:
                        pe.wait_ge(S["hT_ev"], 2 * n + half - 3)
                    for k in range(4):
                        kk = 4 * half + k
                        last = pe.transpose(ps[:, bank, k * P:(k + 1) * P], h[:, ch, kk * P:(kk + 1) * P], C(IDENT))
                    last.then_inc(S["tr_done"], 1)

            def out_rows(l, c, n):
                if c == 3:
                    pe.wait_ge(S["hT_ev"], 4 * CH * l + 2 * CH + n + 1)
                for k in range(KD):
                    last = pe.matmul(ps[:, OUT_BANK[c] + n, :], merged[:, k, c * P:(c + 1) * P],
                                     w_out[:, k, n * 512:(n + 1) * 512], start=(k == 0), stop=(k == KD - 1))
                last.then_inc(S["wo_done"], 1)

            def first_query(l):
                pe.wait_ge(S["hT_ev"], 4 * CH * l + 2 * CH + 2)
                for c in range(2):
                    pe.wait_ge(q_in[c], 16 * l * HEADS + 16)
                    for k in range(KD):
                        last = pe.matmul(ps[:, 6 + c, 0:P], q_w[:, c, k, :], hT[:, k, 0:P],
                                         start=(k == 0), stop=(k == KD - 1))
                    last.then_inc(S["query0_done"], 1)

            def first_scores(l):
                for c in range(2):
                    pe.wait_ge(S["qst0_ev"], 2 * l + c + 1)
                    pe.matmul(ps[:, 6 + c, 0:P], q_st[:, c, 0:P], q_w[:, c, KD, :],
                              start=True, stop=True).then_inc(S["sc0_done"], 1)

            def project(i, g, bank):
                pe.wait_ge(w_in[g], 16 * i + 16)
                for k in range(KD):
                    last = pe.matmul(ps[:, bank, :], w_qkv[:, g, k, :], hT[:, k, :], start=(k == 0), stop=(k == KD - 1))
                last.then_inc(proj[g], 1)

            def query(l, head, c):
                n = (l * HEADS + head) * 2 + c
                pe.wait_ge(q_in[c], 16 * (l * HEADS + head) + 16)
                pe.wait_ge(S["qst_ev"], n + 1)
                for k in range(KD):
                    last = pe.matmul(ps[:, 2 + c, :], q_w[:, c, k, :], hT[:, k, :], start=(k == 0), stop=(k == KD - 1))
                last.then_inc(S["query_done"], 1)

            def head_scores(l, head):
                for c in range(2):
                    n = (l * HEADS + head) * 2 + c
                    pe.wait_ge(S["qst_ev"], n + 3)
                    pe.wait_ge(S["sc_ev"], n + 1)
                    for ch in range(CH):
                        last = pe.matmul(ps[:, 4 + c, ch * P:(ch + 1) * P], q_st[:, c, ch * P:(ch + 1) * P],
                                         q_w[:, c, KD, :], start=True, stop=True)
                    last.then_inc(S["sc_done"], 1)

            def peer_head(l, hd, last_head):
                for ch in range(CH):
                    if not last_head and 1 <= ch <= 2:
                        query(l, hd + 1, ch - 1)
                    if not last_head and ch == CH - 1:
                        head_scores(l, hd + 1)
                    J = (l * HEADS + hd) * CH + ch
                    pe.wait_ge(S["v_added"], J + 1)
                    pe.wait_ge(S["diag_done"], 8 * J + 8)
                    for k in range(V_PE):
                        pe.wait_ge(v_in[k], 32 * J + 16)
                        for n in range(2):
                            last = pe.matmul(ps[:, n, :], diag[:, k, :], ring_v[:, k, n * 512:(n + 1) * 512],
                                             start=(k == 0), stop=(k == V_PE - 1))
                        last.then_inc(S["v_pe"], 1)

            def project_v(g, bank, chunks):
                for c in chunks:
                    for k in range(KD):
                        last = pe.matmul(ps[:, bank, c * P:(c + 1) * P], hT[:, k, c * P:(c + 1) * P],
                                         w_qkv[:, g, k, :], start=(k == 0), stop=(k == KD - 1))
                return last

            def key_products(i, ks):
                for k in ks:
                    last = pe.matmul(ps[:, 1, :], w_qkv[:, 1, k, :], hT[:, k, :], start=(k == 0), stop=(k == KD - 1))
                return last

            def mix(i, last_turn):
                pe.wait_ge(S["dq_ready"], i + 1)
                project(i, 0, 0)
                n0 = FIRST_BLOCKS + TURN_BLOCKS * i
                mod_block(n0, 0)
                pe.wait_ge(w_in[2], 16 * i + 16)
                pe.wait_ge(S["yd_ev"], i + 1)
                project_v(2, 7, range(CH)).then_inc(proj[2], 1)
                mod_block(n0 + 1, 1)

                def piece(u):
                    if u == 0:
                        pe.wait_ge(S["q_ev"], i + 1)
                        project(i, 3, 0)
                    if u == 2:
                        pe.wait_ge(S["k_ev"], i + 1)
                        project(i, 4, 1)
                    if u == 6:
                        pe.wait_ge(w_in[5], 16 * i + 16)
                        pe.wait_ge(S["v_ev"], i + 1)
                        project_v(5, 7, [0])
                    if u == 7:
                        project_v(5, 7, [1]).then_inc(S["dv_mm"], 1)
                    if u == 5:
                        pe.wait_ge(S["dqraw_ev"], i + 1)
                        pe.matmul(ps[:, 0, :], C(ROPE_PERM), dq_raw, start=True, stop=True).then_inc(S["rope_mm"], 1)
                    if u == 6:
                        pe.wait_ge(S["dkraw_ev"], i + 1)
                        pe.matmul(ps[:, 1, :], C(ROPE_PERM), dk_raw, start=True, stop=True).then_inc(S["rope_mm"], 1)

                def logits(u, bank, stop):
                    h, kb = u // CH, CH - 1 - u % CH
                    r = slice(HD * h, HD * h + HD)
                    return pe.matmul(ps[:, bank, 0:qcols(kb)], sb_k[r, kb * P:(kb + 1) * P], sb_q[r, kb * P:SEQ],
                                     start=True, stop=stop)

                for u in range(2 * CH + 2):
                    if u == 1:
                        mod_block(n0 + 2, 2)
                    if u < 2 * CH:
                        if u == 0:
                            pe.wait_ge(S["q_ev"], i + 1)
                            pe.wait_ge(S["k_ev"], i + 1)
                        if u < 2:
                            pe.wait_ge(S["p_exp"], 8 * i + 1)
                        else:
                            pe.wait_ge(S["L_done"], 8 * i + u - 1)
                        logits(u, 2 + u % 2, True).then_inc(S["z_done"], 1)
                        piece(u)
                    if 1 <= u <= 2 * CH:
                        b = u - 1
                        h, kb = b // CH, CH - 1 - b % CH
                        pe.wait_ge(S["L_done"], 8 * i + b + 1)
                        if b < 2:
                            pe.wait_ge(S["wt_ev"], CH * i + 1)
                        else:
                            pe.wait_ge(S["w_exp"], 8 * i + b - 1)
                        bank = 4 + b % 2
                        logits(b, bank, False)
                        last = pe.matmul(ps[:, bank, 0:qcols(kb)], C(NEG_UPPER), L[:, h, kb, 0:qcols(kb)],
                                         start=False, stop=(kb == CH - 1))
                        for kk in range(kb + 1, CH):
                            last = pe.matmul(ps[:, bank, (kk - kb) * P:qcols(kb)], C(NEG_ONES),
                                             L[:, h, kk, 0:qcols(kk)], start=False, stop=(kk == CH - 1))
                        last.then_inc(S["b_done"], 1)
                    if u >= 2:
                        b = u - 2
                        h, kb = b // CH, CH - 1 - b % CH
                        pe.wait_ge(S["w_masked"], 8 * i + b + 1)
                        if b == 0:
                            pe.wait_ge(S["v_ev"], i + 1)
                            pe.wait_ge(S["mod_evac"], n0 + TURN_BLOCKS)
                        pe.matmul(ps[HD * h:HD * h + HD, 6, kb * P:SEQ], sb_v[:, kb * P + HD * h:kb * P + HD * h + HD],
                                  w_att[:, b % 2, 0:qcols(kb)], start=(kb == CH - 1), stop=(kb == 0),
                                  skip_group_check=True).then_inc(S["pv_done"], 1)

                pe.wait_ge(S["dq_ready"], i + 2)
                pe.wait_ge(S["dk_ready"], i + 2)
                for step in range(CH + 3):
                    if step < CH:
                        for c in range(2):
                            v = 2 * step + c
                            if v >= 2:
                                pe.wait_ge(S["p_exp"], 8 * i + v)
                            r = slice(HD * c, HD * c + HD)
                            pe.matmul(ps[:, 2 + c, 0:(step + 1) * P], dq[r, step * P:(step + 1) * P],
                                      dk[r, 0:(step + 1) * P], start=True, stop=True).then_inc(S["s_done"], 1)
                    if step == 0:
                        pe.wait_ge(S["dv_ev"], 2 * i + 1)
                        project_v(5, 7, [2])
                    if step == 1:
                        project_v(5, 7, [3]).then_inc(proj[5], 1)
                    if 2 <= step < CH + 1 and not last_turn:
                        if step == 2:
                            pe.wait_ge(w_in[1], 16 * i + 32)
                        key_products(i + 1, [2 * step - 4])
                    if 1 <= step <= CH:
                        q = step - 1
                        pe.wait_ge(S["dw_done"], CH * i + q + 1)
                        if q < 2:
                            pe.wait_ge(S["w_exp"], 8 * i + 8)
                        else:
                            pe.wait_ge(S["wt_ev"], CH * i + q)
                        for kb in range(q + 1):
                            last = pe.transpose(ps[:, 4 + q % 2, kb * P:(kb + 1) * P],
                                                prob[:, 2 * (q % 2), kb * P:(kb + 1) * P], C(IDENT))
                        last.then_inc(S["wt_done"], 1)
                    if 2 <= step < CH + 1 and not last_turn:
                        key_products(i + 1, [2 * step - 3])
                    if step == CH + 1 and not last_turn:
                        key_products(i + 1, [6])
                    if 2 <= step <= CH + 1:
                        q = step - 2
                        pe.wait_ge(S["wt_ev"], CH * i + q + 2)
                        if q == 0:
                            pe.wait_ge(S["ysb_ev"], i + 1)
                            pe.wait_ge(S["dv_ev"], 2 * i + 1)
                        if q == 2:
                            pe.wait_ge(S["dv_ev"], 2 * i + 2)
                        for kb in range(q + 1):
                            last = pe.matmul(ps[:, Y_BANK[q], q * P:(q + 1) * P], w_t[:, q % 2, kb * P:(kb + 1) * P],
                                             d_v[:, kb * P:(kb + 1) * P], start=(kb == 0), stop=(kb == q))
                        last.then_inc(S["y_done"], 1)
                    if step == CH + 1 and not last_turn:
                        key_products(i + 1, [7]).then_inc(proj[1], 1)
                    if step >= 3:
                        q = step - 3
                        pe.wait_ge(S["yn_done"], CH * i + q + 1)
                        if q == 0:
                            pe.wait_ge(S["dv_ev"], 2 * i + 2)
                        pe.transpose(ps[:, 7, q * P:(q + 1) * P], y_n[:, q % 2, :], C(IDENT)).then_inc(S["yt_done"], 1)

            for n in range(FIRST_BLOCKS):
                mod_block(n, n % TURN_BLOCKS)
            pe.wait_ge(S["const_in"], 4 * 16)
            with pe.Fori(0, DEPTH) as l:
                for ch in range(CH):
                    transposes(l, 0, ch, h1)
                pe.wait_ge(S["hT_ev"], 4 * CH * l + 2 * CH)
                park()
                project(l * TURNS, 1, 1)
                with pe.Fori(0, TURNS - 1) as t:
                    mix(l * TURNS + t, False)
                mix(l * TURNS + TURNS - 1, True)
                pe.wait_ge(S["yd_ev"], TURNS * l + TURNS + 1)
                park()
                with pe.Fori(0, MT // 2) as m2:
                    for s in range(2):
                        m = l * MT + m2 * 2 + s
                        pe.wait_ge(m_in[s], 16 * (l * (MT // 2) + m2) + 16)
                        pe.wait_ge(S["merged_done"], m + 1)
                        for b, (k0, n, rhs) in enumerate(((0, KD, hT), (KD, KD, hT), (16, 4, y_sb), (20, 4, y_d))):
                            for k in range(n):
                                last = pe.matmul(ps[:, 4 * s + b, :], w_m[:, s, k0 + k, :], rhs[:, k, :],
                                                 start=(k == 0), stop=(k == n - 1))
                            last.then_inc(m_mm[s], 1)
                pe.wait_ge(S["merged_done"], MT * l + MT + 2)
                pe.wait_ge(S["wout_in"], 64 * l + 64)
                out_rows(l, 0, 0)
                out_rows(l, 0, 1)
                out_rows(l, 1, 0)
                transposes(l, 1, 0, h2)
                out_rows(l, 1, 1)
                first_query(l)
                out_rows(l, 2, 0)
                first_scores(l)
                out_rows(l, 2, 1)
                transposes(l, 1, 1, h2)
                out_rows(l, 3, 0)
                out_rows(l, 3, 1)
                transposes(l, 1, 2, h2)
                transposes(l, 1, 3, h2)
                pe.wait_ge(S["hT_ev"], 4 * CH * l + 4 * CH)
                park()
                query(l, 0, 0)
                query(l, 0, 1)
                head_scores(l, 0)
                with pe.Fori(0, HEADS - 1) as hd:
                    peer_head(l, hd, False)
                peer_head(l, HEADS - 1, True)

        @block.scalar
        def _(act):
            def park():
                act.sem_inc(S["parked_act"], 1)

            def start_root(dst, total, n):
                act.drain()
                act.activation(dst, total, ACT.Ln, scale=1.0 / n, bias=eps[:, :])
                act.drain()
                return act.activation(dst, dst, ACT.Exp, scale=-0.5)

            act.sem_inc(S["p_exp"], 1)
            act.sem_inc(S["wt_ev"], 1)
            act.sem_inc(S["yd_ev"], 1)
            act.sem_inc(S["qst_ev"], 2)
            act.sem_inc(S["sc_ev"], 2)
            act.wait_ge(S["c_in"], 16)
            act.activation(c_sig[:, :], c_raw[:, :], ACT.Sigmoid).then_inc(S["c_sig_done"], 1)

            def mod_evac(n, place):
                act.wait_ge(S["mod_mm"], n + 1)
                park()
                act.copy(mod[:, :, :].rearrange("p a d -> p (a d)")[:, bass.ds(place * 512, 512)],
                         ps[:, 6, :]).then_inc(S["mod_evac"], 1)

            def square_sum(ch):
                act.activation(h_row[:, :], x[:, ch, :], ACT.Square, accum_out=ss[:, ch:ch + 1])
                act.drain()

            def hT_out(l, which, ch):
                for half in range(2):
                    act.wait_ge(S["tr_done"], 2 * (l * 2 * CH + which * CH + ch) + half + 1)
                    act.copy(hT[:, 4 * half:4 * half + 4, ch * P:(ch + 1) * P],
                             ps[:, TR_BANK[ch] + half, :].rearrange("p (k n) -> p k n", k=4)).then_inc(S["hT_ev"], 1)

            def norm1(l):
                for ch in range(CH):
                    square_sum(ch)
                start_root(root0[:, :], ss[:, :], D).then_inc(S["sq_done"], 1)
                for ch in range(CH):
                    hT_out(l, 0, ch)

            def norm2(l):
                for ch in range(CH):
                    act.wait_ge(S["x_upd"], 2 * CH * l + 2 * ch + 2)
                    square_sum(ch)
                    start_root(root0[:, ch:ch + 1], ss[:, ch:ch + 1], D).then_inc(S["sq2_done"], 1)
                    if ch == 1:
                        for c in range(2):
                            act.wait_ge(S["sc0_done"], 2 * l + c + 1)
                            act.copy(scores[:, 0, c, :], ps[:, 6 + c, 0:P]).then_inc(S["sc0_ev"], 1)
                    if ch < 2:
                        hT_out(l, 1, ch)
                    if ch == 0:
                        for c in range(2):
                            act.wait_ge(S["query0_done"], 2 * l + c + 1)
                            act.copy(q_st[:, c, 0:P], ps[:, 6 + c, 0:P]).then_inc(S["qst0_ev"], 1)
                hT_out(l, 1, 2)
                hT_out(l, 1, 3)

            def stage_query(l, head, c):
                n = (l * HEADS + head) * 2 + c
                act.wait_ge(S["query_done"], n + 1)
                act.wait_ge(S["sc_done"], n + 1)
                act.copy(q_st[:, c, :], ps[:, 2 + c, :]).then_inc(S["qst_ev"], 1)

            def stage_scores(l, head, ch0):
                for c in range(2):
                    act.wait_ge(S["sc_done"], (l * HEADS + head) * 2 + c + 3)
                    act.copy(scores[:, ch0:CH, c, :], ps[:, 4 + c, ch0 * P:SEQ].rearrange("p (c n) -> p c n", c=CH - ch0)
                             ).then_inc(S["sc_ev"], 1)

            def gates(J):
                act.wait_ge(S["topk_done"], J + 1)
                act.activation(gexp, best, ACT.Exp, bias=nbest, accum_out=gsum).then_inc(S["gate_exp"], 1)

            def peer_head(l, hd, last_head):
                for ch in range(CH):
                    J = (l * HEADS + hd) * CH + ch
                    if not last_head and 1 <= ch <= 2:
                        stage_query(l, hd + 1, ch - 1)
                    if not last_head and ch == CH - 1:
                        stage_scores(l, hd + 1, 0)
                    act.wait_ge(S["dots_done"], J + 1)
                    act.activation(gel, dots, ACT.Gelu).then_inc(S["gelu_done"], 1)
                    act.wait_ge(S["coef_done"], J + 1)
                    act.wait_ge(S["v_pe"], 8 * J + 1)
                    for k in range(V_PE):
                        act.activation(diag[:, k, :], C(IDENT), ACT.Copy, scale=coef[:, k:k + 1]).then_inc(S["diag_done"], 1)
                    if not (last_head and ch == CH - 1):
                        gates(J + 1)

            def mix(i, t):
                act.wait_ge(proj[0], i + 2)
                act.mul(sb_q, ps[:, 0, :], SCALE).then_inc(S["q_ev"], 1)
                n0 = FIRST_BLOCKS + TURN_BLOCKS * i
                mod_evac(n0, TURN_BLOCKS * t)
                act.wait_ge(proj[2], i + 2)
                act.copy(sb_v, ps[:, 7, :]).then_inc(S["v_ev"], 1)
                mod_evac(n0 + 1, TURN_BLOCKS * t + 1)
                for u in range(2 * CH + 1):
                    if u == 1:
                        mod_evac(n0 + 2, TURN_BLOCKS * t + 2)
                    if u < 2 * CH:
                        n = qcols(CH - 1 - u % CH)
                        act.wait_ge(S["z_done"], 8 * i + u + 1)
                        if u >= 2:
                            act.wait_ge(S["L_done"], 8 * i + u - 1)
                        act.activation(soft[:, u % 2, 0:n], ps[:, 2 + u % 2, 0:n], ACT.Abs)
                        act.drain()
                        act.activation(soft[:, u % 2, 0:n], soft[:, u % 2, 0:n], ACT.Exp, scale=-1.0)
                        act.drain()
                        act.activation(soft[:, u % 2, 0:n], soft[:, u % 2, 0:n], ACT.Ln, bias=1.0).then_inc(S["ln_done"], 1)
                    if u == 2:
                        act.wait_ge(proj[3], i + 2)
                        act.mul(dq_raw, ps[:, 0, :], SCALE).then_inc(S["dqraw_ev"], 1)
                    if u == 4:
                        act.wait_ge(proj[4], i + 2)
                        act.copy(dk_raw, ps[:, 1, :]).then_inc(S["dkraw_ev"], 1)
                    if u >= 1:
                        b = u - 1
                        n = qcols(CH - 1 - b % CH)
                        act.wait_ge(S["b_done"], 8 * i + b + 1)
                        act.wait_ge(S["pv_done"], 8 * i + b + 1)
                        act.activation(w_att[:, b % 2, 0:n], ps[:, 4 + b % 2, 0:n], ACT.Exp).then_inc(S["w_exp"], 1)
                act.wait_ge(S["dv_mm"], i + 1)
                act.copy(d_v[:, 0:2 * P], ps[:, 7, 0:2 * P]).then_inc(S["dv_ev"], 1)
                for step in range(CH + 2):
                    if step == 2:
                        act.wait_ge(proj[5], i + 2)
                        act.copy(d_v[:, 2 * P:SEQ], ps[:, 7, 2 * P:SEQ]).then_inc(S["dv_ev"], 1)
                    if step < CH:
                        for c in range(2):
                            v = 2 * step + c
                            n = (step + 1) * P
                            act.wait_ge(S["max_done"], 8 * i + v + 1)
                            if step >= 2:
                                act.wait_ge(S["wt_done"], CH * i + step - 1)
                            act.activation(prob[:, 2 * (step % 2) + c, 0:n], ps[:, 2 + c, 0:n], ACT.Exp,
                                           bias=nmax[:, v:v + 1], accum_out=zsum[:, v:v + 1]).then_inc(S["p_exp"], 1)
                    if 1 <= step <= CH:
                        q = step - 1
                        act.wait_ge(S["wt_done"], CH * i + q + 1)
                        act.wait_ge(S["y_done"], CH * i + q + 1)
                        act.copy(w_t[:, q % 2, 0:(q + 1) * P], ps[:, 4 + q % 2, 0:(q + 1) * P]).then_inc(S["wt_ev"], 1)
                    if step >= 2:
                        q = step - 2
                        act.wait_ge(S["y_done"], CH * i + q + 3)
                        act.activation(junk_y, ps[:, Y_BANK[q], q * P:(q + 1) * P], ACT.Square,
                                       accum_out=yss[:, q:q + 1])
                        start_root(yroot0[:, q:q + 1], yss[:, q:q + 1], P).then_inc(S["y_sq"], 1)
                act.wait_ge(S["yt_done"], CH * i + CH)
                park()
                act.copy(y_d[:, bass.ds(t, 1), :].rearrange("p a n -> p (a n)"), ps[:, 7, :]).then_inc(S["yd_ev"], 1)

            act.preload_act_table_set("natural_log_exp_and_others")
            for n in range(FIRST_BLOCKS):
                mod_evac(n, MOD_BLOCKS - FIRST_BLOCKS + n)
            act.wait_ge(S["const_in"], 4 * 16)
            act.wait_ge(S["x_in"], 16)
            with act.Fori(0, DEPTH) as l:
                act.wait_ge(S["layer_done"], l + 1)
                park()
                act.preload_act_table_set("natural_log_exp_and_others")
                norm1(l)
                act.wait_ge(S["lam_summed"], l + 1)
                act.activation(lam_exp[:, :], lam_sum[:, :], ACT.Exp).then_inc(S["lam_exped"], 1)
                with act.Fori(0, TURNS) as t:
                    mix(l * TURNS + t, t)
                with act.Fori(0, MT // 2) as m2:
                    for s in range(2):
                        m = l * MT + m2 * 2 + s
                        act.wait_ge(S["merged_done"], m + 1)
                        for b in range(2):
                            act.wait_ge(m_mm[s], 4 * (l * (MT // 2) + m2) + b + 5)
                            park()
                            act.activation(sig[:, s, b, :], ps[:, 4 * s + b, :], ACT.Sigmoid,
                                           bias=gate_b[:, bass.ds(b * MT + m2 * 2 + s, 1)]).then_inc(S["sig_done"], 1)
                act.preload_act_table_set("natural_log_exp_and_others")
                norm2(l)
                gates(l * HEADS * CH)
                stage_query(l, 0, 0)
                stage_query(l, 0, 1)
                stage_scores(l, 0, 1)
                with act.Fori(0, HEADS - 1) as hd:
                    peer_head(l, hd, False)
                peer_head(l, HEADS - 1, True)
            act.preload_act_table_set("natural_log_exp_and_others")
            act.wait_ge(S["layer_done"], DEPTH + 1)
            for ch in range(CH):
                act.activation(h_row[:, :], x[:, ch, :], ACT.Square, accum_out=ss[:, ch:ch + 1])
                act.drain()
            start_root(root0[:, :], ss[:, :], D).then_inc(S["out_sq"], 1)

        @block.gpsimd
        def _(pool):
            def park():
                pool.sem_inc(S["parked_pool"], 1)

            with pool.Fori(0, DEPTH) as l:
                with pool.Fori(0, TURNS) as t:
                    i = l * TURNS + t
                    for u in range(2 * CH):
                        pool.wait_ge(S["w_exp"], 8 * i + u + 1)
                        park()
                        pool.affine_select(out=w_att[:, u % 2, 0:P], in_=w_att[:, u % 2, 0:P], compare_op=ALU.is_gt,
                                           fill=0.0, base=0, pattern=[[1, P]], channel_multiplier=-1
                                           ).then_inc(S["w_masked"], 1)
                with pool.Fori(0, CH * HEADS) as j:
                    J = l * CH * HEADS + j
                    pool.wait_ge(S["topk_done"], J + 1)
                    pool.wait_ge(S["u_used"], 2 * RING * J + RING)
                    park()
                    pool.tensor_copy(idx_u[:, :], idx_next[:, :]).then_inc(S["idx_u_set"], 1)
                    pool.wait_ge(S["idx_u_set"], J + 1)
                    for k in range(TOPK):
                        pool.wait_ge(S["u_used"], TOPK * J + k + 1)
                        park()
                        pool.indirect_dma_start(out=ring_u[:, k % RING, :], out_offset=None, in_=io["u"],
                                                in_offset=bass.IndirectOffsetOnAxis(ap=idx_u[:, k:k + 1], axis=0)
                                                ).then_inc(u_in[k % RING], 16)
                    pool.wait_ge(S["v_dve"], RING * J + RING)
                    park()
                    pool.tensor_copy(idx_v[:, :], idx_next[:, :]).then_inc(S["idx_taken"], 1)
                    pool.wait_ge(S["idx_taken"], J + 1)
                    for k in range(TOPK):
                        if k < RING:
                            pool.wait_ge(S["v_dve"], RING * J + k + 1)
                        else:
                            pool.wait_ge(S["v_pe"], RING * J + k - RING + 2)
                        park()
                        pool.indirect_dma_start(out=ring_v[:, k % RING, :], out_offset=None, in_=io["v"],
                                                in_offset=bass.IndirectOffsetOnAxis(ap=idx_v[:, k:k + 1], axis=0)
                                                ).then_inc(v_in[k % RING], 16)

        @block.vector
        def _(dve):
            def park():
                dve.sem_inc(S["parked_dve"], 1)

            dve.memset(ones[:, :], 1.0)
            dve.memset(eps[:, :], EPS)
            for i in range(DEPTH):
                dve.memset(lam_init[:, i:i + 1], LAM_INIT[i])
                dve.memset(lam_rest[:, i:i + 1], 1.0 - LAM_INIT[i])
                dve.memset(expert0[:, i:i + 1], float(i * N_EXPERTS))
            for name, n in (("layer_done", 1), ("norm_gain", 1), ("dq_ready", 1), ("dk_ready", 1),
                            ("merged_done", 2), ("v_added", 1), ("u_used", RING), ("v_dve", RING)):
                dve.sem_inc(S[name], n)
            dve.memset(bias_first, 0.0).then_inc(S["zeros_done"], 1)
            dve.wait_ge(S["c_sig_done"], 1)
            dve.tensor_tensor(c_act[:, :], c_sig[:, :], c_raw[:, :], ALU.mult)
            dve.drain().then_inc(S["c_act_done"], 1)

            def mod_acc_block(turn, b, slot, bias):
                for half in range(2):
                    at = 2 * b + half
                    dve.wait_ge(ada_in[at % 3], 16 * (2 * turn + at // 3) + 16)
                    cols = slice(half * 256, half * 256 + 256)
                    acc = mod_acc[:, slot, cols]
                    for k in range(KD):
                        last = dve.scalar_tensor_tensor(acc, ada_w[at % 3][:, k, :], c_act[:, k:k + 1],
                                                        bias[:, cols] if k == 0 else acc, ALU.mult, ALU.add)
                        if k < KD - 1:
                            dve.drain()
                    last.then_inc(S["acc_done"], 1)

            def inv_root_mean(dst, start, total, n):
                width = dst.shape[-1]
                a, b = newton[:, 0, 0:width], newton[:, 1, 0:width]
                dve.tensor_scalar(a, total, 1.0 / n, EPS, ALU.mult, ALU.add)
                dve.tensor_tensor(b, start, start, ALU.mult)
                dve.drain()
                dve.tensor_tensor(a, a, b, ALU.mult)
                dve.drain()
                dve.tensor_scalar(a, a, -0.5, 1.5, ALU.mult, ALU.add)
                dve.drain()
                dve.tensor_tensor(dst, start, a, ALU.mult)
                dve.drain()

            def norm_gain(l, which):
                gain = mod[:, GAIN2 if which else GAIN1, :]
                dve.wait_ge(S["g_in"], 32 * l + 16 * which + 16)
                dve.wait_ge(S["mod_evac"], l * MOD_BLOCKS + (MOD_BLOCKS if which else 0) + FIRST_BLOCKS)
                dve.scalar_tensor_tensor(gain, gain, 1.0, g_row[:, :], ALU.add, ALU.mult).then_inc(S["norm_gain"], 1)

            def norm_rows(ch, which, h):
                shift, gain = (mod[:, SHIFT2, :], mod[:, GAIN2, :]) if which else (mod[:, SHIFT1, :], mod[:, GAIN1, :])
                dve.scalar_tensor_tensor(h[:, ch, :], x[:, ch, :], rstd[:, ch:ch + 1], gain, ALU.mult, ALU.mult)
                dve.drain()
                dve.tensor_tensor(h[:, ch, :], h[:, ch, :], shift, ALU.add).then_inc(S["norm_h"], 1)

            def rope(i, which, raw, dst, bank, done):
                if which:
                    dve.wait_ge(S["dkraw_ev"], i + 1)
                else:
                    dve.wait_ge(S["dqraw_ev"], i + 1)
                dve.tensor_tensor(rope_tmp[:, 0, :], raw, cos_t[:, :], ALU.mult)
                dve.wait_ge(S["rope_mm"], 2 * i + which + 1)
                dve.tensor_tensor(rope_tmp[:, 1, :], ps[:, bank, :], sin_t[:, :], ALU.mult)
                dve.drain()
                dve.tensor_tensor(dst, rope_tmp[:, 0, :], rope_tmp[:, 1, :], ALU.add).then_inc(S[done], 1)
                dve.drain()

            def mix(i, t):
                dve.wait_ge(S["bias_in"], 16 * i + 32)
                for b in range(TURN_BLOCKS):
                    mod_acc_block(i, FIRST_BLOCKS + b, b, bias0[:, b, :])
                    if b == 0:
                        dve.wait_ge(proj[1], i + 2)
                        dve.tensor_copy(sb_k, ps[:, 1, :]).then_inc(S["k_ev"], 1)
                for u in range(2 * CH + 1):
                    if u >= 1:
                        b = u - 1
                        h, kb = b // CH, CH - 1 - b % CH
                        n = qcols(kb)
                        dve.wait_ge(S["ln_done"], 8 * i + b + 1)
                        dve.scalar_tensor_tensor(L[:, h, kb, 0:n], ps[:, 2 + b % 2, 0:n], 0.0, soft[:, b % 2, 0:n],
                                                 ALU.max, ALU.add)
                        dve.drain()
                        dve.tensor_tensor(L[:, h, kb, 0:P], L[:, h, kb, 0:P], C(STRICT), ALU.mult).then_inc(S["L_done"], 1)
                        dve.drain()
                    if u == 6:
                        rope(i, 0, dq_raw, dq, 0, "dq_ready")
                    if u == 7:
                        rope(i, 1, dk_raw, dk, 1, "dk_ready")
                dve.wait_ge(S["pv_done"], 8 * i + 8 + 2)
                dve.tensor_copy(y_sb[:, bass.ds(t, 1), :].rearrange("p a n -> p (a n)"), ps[:, 6, :]).then_inc(S["ysb_ev"], 1)
                for step in range(CH + 3):
                    if step < CH:
                        for c in range(2):
                            v = 2 * step + c
                            dve.wait_ge(S["s_done"], 8 * i + v + 1)
                            dve.tensor_tensor(ps[:, 2 + c, step * P:(step + 1) * P], ps[:, 2 + c, step * P:(step + 1) * P],
                                              C(NEG_MASK), ALU.add)
                            dve.drain()
                            dve.tensor_reduce(nmax[:, v:v + 1], ps[:, 2 + c, 0:(step + 1) * P], AX.X, ALU.max,
                                              negate=True).then_inc(S["max_done"], 1)
                    if 1 <= step <= CH:
                        q = step - 1
                        n = (q + 1) * P
                        p0, p1 = prob[:, 2 * (q % 2), 0:n], prob[:, 2 * (q % 2) + 1, 0:n]
                        dve.wait_ge(S["p_exp"], 8 * i + 2 * q + 3)
                        dve.reciprocal(rz[:, 2 * q:2 * q + 2], zsum[:, 2 * q:2 * q + 2])
                        dve.drain()
                        dve.tensor_scalar(p1, p1, rz[:, 2 * q + 1:2 * q + 2], neg_lam[:, 0:1], ALU.mult, ALU.mult)
                        dve.drain()
                        dve.scalar_tensor_tensor(p0, p0, rz[:, 2 * q:2 * q + 1], p1, ALU.mult, ALU.add).then_inc(S["dw_done"], 1)
                        dve.drain()
                    if step >= 3:
                        q = step - 3
                        dve.wait_ge(S["y_sq"], CH * i + q + 1)
                        inv_root_mean(yr[:, q:q + 1], yroot0[:, q:q + 1], yss[:, q:q + 1], P)
                        if q >= 2:
                            dve.wait_ge(S["yt_done"], CH * i + q - 1)
                        dve.scalar_tensor_tensor(y_n[:, q % 2, :], ps[:, Y_BANK[q], q * P:(q + 1) * P], yr[:, q:q + 1], g_sub[:, :],
                                                 ALU.mult, ALU.mult).then_inc(S["yn_done"], 1)

            def topk_pair(vals, idxs, src, work):
                dve.max(vals[:, 0:8], src)
                dve.drain()
                dve.max_index(idxs[:, 0:8], vals[:, 0:8], src)
                dve.match_replace(work, vals[:, 0:8], src, LOWEST)
                dve.drain()
                dve.max(vals[:, 8:16], work)
                dve.drain()
                dve.max_index(idxs[:, 8:16], vals[:, 8:16], work)

            def topk(l, ch, count):
                if count is not None:
                    dve.wait_ge(S["idx_taken"], count)
                    dve.wait_ge(S["gate_exp"], count)
                    park()
                for c in range(2):
                    topk_pair(s_top[:, c, :], i_top[:, c, :], scores[:, ch, c, :], sc_work[:, c, :])
                dve.drain()
                dve.tensor_copy(i_top_f, i_top[:, :, :])
                dve.tensor_tensor(cand, s_top[:, 0, :].unsqueeze(2).broadcast_to([P, TOPK, TOPK]),
                                  s_top[:, 1, :].unsqueeze(1).broadcast_to([P, TOPK, TOPK]), ALU.add)
                dve.drain()
                flat = cand.rearrange("p a b -> p (a b)")
                topk_pair(best, pos[:, :], flat, cand_work.rearrange("p a b -> p (a b)"))
                dve.drain()
                dve.tensor_scalar(nbest, best[:, 0:1], -1.0, None, ALU.mult)
                dve.tensor_scalar(pos_hl[:, 0, :], pos[:, :], 4, None, ALU.logical_shift_right)
                dve.tensor_scalar(pos_hl[:, 1, :], pos[:, :], 15, None, ALU.bitwise_and)
                dve.drain()
                dve.tensor_copy(pos_f, pos_hl[:, :, :])
                dve.drain()
                for c in range(2):
                    dve.tensor_tensor(onehot, pos_f[:, c, :].unsqueeze(2).broadcast_to([P, TOPK, TOPK]),
                                      iota16[:, :].unsqueeze(1).broadcast_to([P, TOPK, TOPK]), ALU.is_equal)
                    dve.drain()
                    dve.tensor_tensor(onehot, onehot, i_top_f[:, c, :].unsqueeze(1).broadcast_to([P, TOPK, TOPK]), ALU.mult)
                    dve.drain()
                    dve.tensor_reduce(sel_f[:, c, :], onehot, AX.X, ALU.add)
                    dve.drain()
                dve.scalar_tensor_tensor(sel_f[:, 0, :], sel_f[:, 0, :], float(N_KEYS), sel_f[:, 1, :], ALU.mult, ALU.add)
                dve.drain()
                dve.tensor_scalar(idx_next[:, :], sel_f[:, 0, :], expert0[:, bass.ds(l, 1)], None,
                                  ALU.add).then_inc(S["topk_done"], 1)

            for n in range(FIRST_BLOCKS):
                if n == 0:
                    dve.wait_ge(S["bias_in"], 16)
                if n == TURN_BLOCKS:
                    dve.wait_ge(S["mod_mm"], 1)
                mod_acc_block(0, n, n % TURN_BLOCKS, bias_first[:, n, :])
            dve.wait_ge(S["mod_mm"], FIRST_BLOCKS)
            def peer_head(l, hd, last_head):
                for ch in range(CH):
                    J = (l * HEADS + hd) * CH + ch
                    total = peer_sum[:, ch, :]
                    for k in range(TOPK):
                        dve.wait_ge(u_in[k % RING], 32 * J + 16 * (k // RING) + 16)
                        row = ring_u[:, k % RING, :]
                        dve.tensor_tensor_reduce(row, row, h2[:, ch, :], 1.0, 0.0, ALU.mult, ALU.add,
                                                 dots[:, k:k + 1]).then_inc(S["u_used"], 1)
                    dve.drain().then_inc(S["dots_done"], 1)
                    dve.wait_ge(S["gate_exp"], J + 1)
                    dve.reciprocal(rsum, gsum)
                    dve.drain()
                    dve.wait_ge(S["gelu_done"], J + 1)
                    dve.scalar_tensor_tensor(coef, gel, rsum, gexp, ALU.mult, ALU.mult).then_inc(S["coef_done"], 1)
                    if ch < CH - 1:
                        dve.wait_ge(S["sc_ev"], 2 * (l * HEADS + hd) + 4)
                        topk(l, ch + 1, J + 1)
                    elif not last_head:
                        dve.wait_ge(S["sc_ev"], 2 * (l * HEADS + hd + 1) + 4)
                        topk(l, 0, J + 1)
                    for k in range(V_PE, TOPK):
                        dve.wait_ge(v_in[k % RING], 32 * J + 32)
                        dve.scalar_tensor_tensor(total, ring_v[:, k % RING, :], coef[:, k:k + 1], total,
                                                 ALU.mult, ALU.add).then_inc(S["v_dve"], 1)
                        dve.drain()
                    dve.wait_ge(S["v_pe"], 8 * J + 8 + 1)
                    dve.tensor_tensor(total, total, ps[:, 0:2, :].rearrange("p a n -> p (a n)"),
                                      ALU.add).then_inc(S["v_added"], 1)
                    if last_head:
                        dve.drain()
                        dve.tensor_tensor(total, total, mod[:, GATE2, :], ALU.mult)
                        dve.drain()
                        dve.tensor_tensor(x[:, ch, :], x[:, ch, :], total, ALU.add)

            with dve.Fori(0, DEPTH) as l:
                dve.memset(bias0, 0.0).then_inc(S["zeros_done"], 1)
                dve.wait_ge(S["small_in"], 48 * l + 48)
                for c in range(2):
                    dve.tensor_tensor(lam_prod[:, c, :], lam_raw[:, 2 * c, :], lam_raw[:, 2 * c + 1, :], ALU.mult)
                dve.drain()
                dve.tensor_reduce(lam_sum[:, :], lam_prod[:, :, :], AX.X, ALU.add).then_inc(S["lam_summed"], 1)
                dve.tensor_scalar(g_sub[:, :], g_sub[:, :], lam_rest[:, bass.ds(l, 1)], None, ALU.mult)
                norm_gain(l, 0)
                dve.wait_ge(S["sq_done"], l + 1)
                inv_root_mean(rstd[:, :], root0[:, :], ss[:, :], D)
                for ch in range(CH):
                    norm_rows(ch, 0, h1)
                dve.wait_ge(S["lam_exped"], l + 1)
                dve.tensor_tensor(neg_lam[:, :], lam_exp[:, 1:2], lam_exp[:, 0:1], ALU.subtract)
                dve.drain()
                dve.tensor_tensor(neg_lam[:, :], neg_lam[:, :], lam_init[:, bass.ds(l, 1)], ALU.subtract)
                with dve.Fori(0, TURNS) as t:
                    mix(l * TURNS + t, t)
                with dve.Fori(0, MT // 2) as m2:
                    for s in range(2):
                        m = l * MT + m2 * 2 + s
                        for b in range(2):
                            dve.wait_ge(S["sig_done"], 2 * m + b + 1)
                            dve.wait_ge(m_mm[s], 4 * (l * (MT // 2) + m2) + b + 7)
                            dve.tensor_tensor(sig[:, s, b, :], sig[:, s, b, :], ps[:, 4 * s + 2 + b, :], ALU.mult)
                        dve.drain()
                        dve.tensor_tensor(merged[:, bass.ds(m2 * 2 + s, 1), :].rearrange("p a n -> p (a n)"),
                                          sig[:, s, 0, :], sig[:, s, 1, :], ALU.add).then_inc(S["merged_done"], 1)
                dve.drain()
                norm_gain(l, 1)
                dve.drain()

                def residual(c):
                    for n in range(2):
                        cols = slice(n * 512, (n + 1) * 512)
                        dve.wait_ge(S["wo_done"], 2 * CH * l + 2 * c + n + 1)
                        dve.tensor_tensor(out_tmp, ps[:, OUT_BANK[c] + n, :], mod[:, GATE1, cols], ALU.mult)
                        dve.drain()
                        dve.tensor_tensor(x[:, c, cols], x[:, c, cols], out_tmp, ALU.add).then_inc(S["x_upd"], 1)
                        dve.drain()
                    dve.wait_ge(S["sq2_done"], CH * l + c + 1)
                    inv_root_mean(rstd[:, c:c + 1], root0[:, c:c + 1], ss[:, c:c + 1], D)
                    norm_rows(c, 1, h2)

                for c in range(CH - 1):
                    residual(c)
                dve.wait_ge(S["sc0_ev"], 2 * l + 2)
                park()
                topk(l, 0, None)
                residual(CH - 1)
                dve.memset(peer_sum, 0.0)
                with dve.Fori(0, HEADS - 1) as hd:
                    peer_head(l, hd, False)
                peer_head(l, HEADS - 1, True)
                dve.drain().then_inc(S["layer_done"], 1)

            dve.wait_ge(S["g_in"], 32 * DEPTH + 16)
            dve.wait_ge(S["out_sq"], 1)
            inv_root_mean(rstd[:, :], root0[:, :], ss[:, :], D)
            for ch in range(CH):
                dve.scalar_tensor_tensor(h2[:, ch, :], x[:, ch, :], rstd[:, ch:ch + 1], g_row[:, :],
                                         ALU.mult, ALU.mult).then_inc(S["out_ready"], 1)


def shape_constants():
    i, j = np.arange(P)[:, None], np.arange(P)[None, :]
    const = np.zeros((P, N_CONST, P), np.float32)
    const[:, IDENT] = i == j
    const[:, NEG_UPPER] = -1.0 * (i >= j)
    const[:, NEG_ONES] = -1.0
    const[:, STRICT] = i < j
    const[:, NEG_MASK] = -1e30 * (j > i)
    half = ROT // 2
    in_head = j % HD
    const[:, ROPE_PERM] = (1.0 * ((in_head >= half) & (in_head < ROT) & (i == j - half))
                           - 1.0 * ((in_head < half) & (i == j + half)))
    inv_freq = (1.0 / (np.float32(ROPE_THETA) ** (np.arange(0, ROT, 2, dtype=np.float32) / np.float32(ROT))))
    angle = inv_freq.astype(np.float32)[:, None] * np.arange(SEQ, dtype=np.float32)[None, :]
    cos_t, sin_t = np.ones((P, SEQ), np.float32), np.zeros((P, SEQ), np.float32)
    for p in range(P):
        if p % HD < ROT:
            cos_t[p], sin_t[p] = np.cos(angle[p % half]), np.sin(angle[p % half])
    return {"const": const, "cos": cos_t, "sin": sin_t, "iota16": np.arange(TOPK, dtype=np.float32)}


def lay_out(a):
    L = DEPTH
    w_in = a["w_in"].reshape(L, KD, P, -1)
    groups = w_in[..., :6 * 512].reshape(L, KD, P, 6, TURNS, P)
    gates = w_in[..., 6 * 512:].reshape(L, KD, P, 2, MT, P)
    b_sb = a["w_branch_sb"].reshape(L, 4, P, MT, P)
    b_d = a["w_branch_diff"].reshape(L, 4, P, MT, P)
    w_m = np.concatenate([gates[:, :, :, 0], gates[:, :, :, 1], b_sb, b_d], axis=1)
    wq = a["peer_wq"].reshape(L, KD, P, 2 * HEADS, P).transpose(0, 3, 2, 1, 4)
    sub = a["peer_subkeys"].reshape(L, 2 * HEADS, N_KEYS, P).transpose(0, 1, 3, 2)[:, :, :, None, :]
    ada_w = a["ada_w"].reshape(L, KD, P, 2 * MOD_BLOCKS, 256).transpose(0, 3, 2, 1, 4).reshape(-1, P, KD, 256)
    return {
        "x": a["x"][0],
        "c": a["c"].reshape(KD, P).T,
        "norm_g": np.stack([a["norm1_g"], a["norm2_g"]], axis=1).reshape(2 * L, D),
        "ada_w": np.concatenate([ada_w, ada_w[:2 * FIRST_BLOCKS]]),
        "ada_b": np.concatenate([a["ada_b"].reshape(-1), a["ada_b"][0, :FIRST_BLOCKS * 512]])[None, :],
        "w_qkv": groups.transpose(0, 4, 3, 2, 1, 5).reshape(-1, P, KD, P),
        "w_m": w_m.transpose(0, 3, 2, 1, 4).reshape(-1, P, 24, P),
        "w_out": a["w_out"].reshape(L, KD, P, D).transpose(0, 2, 1, 3),
        "w_q": np.concatenate([wq, sub], axis=3).reshape(-1, P, KD + 1, P),
        "gate_b": a["gate_b"].reshape(L, 2 * MT, P).transpose(0, 2, 1),
        "lam": a["diff_lambda"],
        "g_sub": a["diff_subln_g"],
        "u": a["peer_u"].reshape(L * N_EXPERTS, D),
        "v": a["peer_v"].reshape(L * N_EXPERTS, D),
        "final_g": a["final_g"],
    }


def kernel(**inputs):
    import concourse.bacc as bacc
    from concourse.bass_utils import run_bass_kernel_spmd

    laid = lay_out({n: np.asarray(v) for n, v in inputs.items()})
    laid.update(shape_constants())
    nc = bacc.Bacc("TRN2", target_bir_lowering=False, num_devices=1)
    arrays, io = {}, {}
    for name, a in laid.items():
        a = np.ascontiguousarray(a)
        arrays[f"in_{name}_dram"] = a
        io[name] = nc.dram_tensor(f"in_{name}_dram", a.shape, mybir.dt.from_np(a.dtype), kind="ExternalInput").ap()
    out = nc.dram_tensor("out_dram", (1, SEQ, D), F32, kind="ExternalOutput").ap()
    build(nc, io, out)
    r = run_bass_kernel_spmd(nc, [arrays], core_ids=[0])
    return r.results[0]["out_dram"]
```
